# Optimizing a Trainium2 kernel written in Bass

```python
import jax, jax.numpy as jnp
from jax import lax
import numpy as np

D_MODEL = 1024
BATCH = 1
SEQ = 256
DEPTH = 1
DEC_BATCH = 8
DEC_SEQ = 1
PAST_LEN = 2048
PAGE_SIZE = 128

D_HEAD = 64
H_RWKV = 8
H_ATT = 8
W_RWKV = H_RWKV * D_HEAD
W_ATT = H_ATT * D_HEAD
D_DECAY_LORA = 64
D_AAA_LORA = 64
D_GATE_LORA = 128
W_RWKV_IN = 3 * W_RWKV + D_DECAY_LORA + D_AAA_LORA + D_GATE_LORA
W_IN = W_RWKV_IN + 3 * W_ATT
GN_EPS = 64e-5
NORM_EPS = 1e-6
MOBA_BLOCK = 256
MOBA_TOPK = 3
Q_CHUNK = 64
ROT_DIM = D_HEAD // 4
ROPE_THETA = 500000.0
PEER_HEADS = 8
PEER_NKEYS = 128
PEER_EXPERTS = PEER_NKEYS * PEER_NKEYS
PEER_TOPK = 16
PEER_DQ = 256
PEER_CHUNK = 256

kernel_name = 'hybrid_rwkv7_moba_peer_step'

def rms_norm(x, g):
    x32 = x.astype(jnp.float32)
    y = x32 * lax.rsqrt(jnp.mean(x32 * x32, axis=-1, keepdims=True) + NORM_EPS)
    return (y * g.astype(jnp.float32)).astype(x.dtype)

def partial_rope(x, pos):
    half = ROT_DIM // 2
    inv = 1.0 / (ROPE_THETA ** (jnp.arange(half, dtype=jnp.float32) * 2.0 / ROT_DIM))
    ang = pos.astype(jnp.float32)[:, None] * inv[None, :]
    cos = jnp.cos(ang)[None, :, None, :]
    sin = jnp.sin(ang)[None, :, None, :]
    x32 = x.astype(jnp.float32)
    x1 = x32[..., :half]
    x2 = x32[..., half:ROT_DIM]
    out = jnp.concatenate([x1 * cos - x2 * sin, x2 * cos + x1 * sin, x32[..., ROT_DIM:]], axis=-1)
    return out.astype(x.dtype)

def project(x, norm_g, w_in, pos):
    b, t, _ = x.shape
    p = rms_norm(x, norm_g) @ w_in
    q, k, v = jnp.split(p[..., W_RWKV_IN:], 3, axis=-1)
    heads = lambda z: z.reshape(b, t, H_ATT, D_HEAD)
    return p[..., :W_RWKV_IN], partial_rope(heads(q), pos), partial_rope(heads(k), pos), heads(v)

def rwkv_group(p, prev0, s0, mu, w0, w_dec, a0, w_aaa, w_gate, k_k, k_a, r_k, gn_g, gn_b):
    f32 = jnp.float32
    b, t, _ = p.shape
    prev = jnp.concatenate([prev0[:, None, :].astype(p.dtype), p[:, :-1]], axis=1)
    ps = p + (prev - p) * mu
    cut = [W_RWKV, 2 * W_RWKV, 3 * W_RWKV, 3 * W_RWKV + D_DECAY_LORA, 3 * W_RWKV + D_DECAY_LORA + D_AAA_LORA]
    r, k, v, wd, ad, gd = jnp.split(ps, cut, axis=-1)
    logw = -jnp.exp(-jax.nn.softplus(-(w0 + jnp.tanh(wd) @ w_dec).astype(f32)) - 0.5)
    a = jax.nn.sigmoid((a0 + ad @ w_aaa).astype(f32))
    g = (jax.nn.sigmoid(gd) @ w_gate).astype(f32)
    hd = lambda z: z.astype(f32).reshape(b, t, H_RWKV, D_HEAD)
    r, k, v, a, decay = hd(r), hd(k), hd(v), hd(a), jnp.exp(hd(logw))
    kk = k * k_k.astype(f32).reshape(H_RWKV, D_HEAD)
    kk = kk / jnp.maximum(jnp.sqrt(jnp.sum(kk * kk, axis=-1, keepdims=True)), 1e-12)
    k = k * (1.0 + (a - 1.0) * k_a.astype(f32).reshape(H_RWKV, D_HEAD))

    def step(s, xs):
        r_t, w_t, k_t, v_t, kk_t, a_t = xs
        sa = jnp.einsum('bhvk,bhk->bhv', s, -kk_t)
        s = s * w_t[:, :, None, :] + sa[..., None] * (kk_t * a_t)[:, :, None, :] + v_t[..., None] * k_t[:, :, None, :]
        return s, jnp.einsum('bhvk,bhk->bhv', s, r_t)

    tm = lambda z: jnp.moveaxis(z, 1, 0)
    s_fin, ys = lax.scan(step, s0.astype(f32), (tm(r), tm(decay), tm(k), tm(v), tm(kk), tm(a)))
    y = jnp.moveaxis(ys, 0, 1)
    mean = jnp.mean(y, axis=-1, keepdims=True)
    var = jnp.mean(jnp.square(y - mean), axis=-1, keepdims=True)
    yn = ((y - mean) * lax.rsqrt(var + GN_EPS)).reshape(b, t, W_RWKV) * gn_g.astype(f32) + gn_b.astype(f32)
    bonus = (jnp.sum(r * k * r_k.astype(f32), axis=-1, keepdims=True) * v).reshape(b, t, W_RWKV)
    out = ((yn + bonus) * g).astype(p.dtype)
    return out, s_fin, p[:, -1]

def moba_attend(q, k_own, v_own, own_mask, k_sel, v_sel, sel_mask):
    scale = D_HEAD ** -0.5
    s_own = jnp.einsum('bqhd,bkhd->bqhk', q, k_own).astype(jnp.float32) * scale
    s_own = jnp.where(own_mask[None, :, None, :], s_own, -jnp.inf)
    if k_sel is None:
        p = jax.nn.softmax(s_own, axis=-1).astype(v_own.dtype)
        return jnp.einsum('bqhk,bkhd->bqhd', p, v_own)
    s_sel = jnp.einsum('bqhd,bqhskd->bqhsk', q, k_sel).astype(jnp.float32) * scale
    s_sel = jnp.where(sel_mask[..., None], s_sel, -jnp.inf)
    n_s = s_sel.shape[3] * s_sel.shape[4]
    scores = jnp.concatenate([s_sel.reshape(s_sel.shape[:3] + (n_s,)), s_own], axis=-1)
    p = jax.nn.softmax(scores, axis=-1).astype(v_own.dtype)
    p_sel = p[..., :n_s].reshape(s_sel.shape)
    return jnp.einsum('bqhsk,bqhskd->bqhd', p_sel, v_sel) + jnp.einsum('bqhk,bkhd->bqhd', p[..., n_s:], v_own)

def moba_prompt(q, k, v):
    b, t, h, dh = q.shape
    nb = -(-t // MOBA_BLOCK)
    tp = nb * MOBA_BLOCK
    padw = ((0, 0), (0, tp - t), (0, 0), (0, 0))
    kp = jnp.pad(k, padw)
    vp = jnp.pad(v, padw)
    n_sel = min(MOBA_TOPK, nb - 1)
    qblk = jnp.arange(t) // MOBA_BLOCK
    bi = jnp.arange(b)[:, None, None, None]
    hi = jnp.arange(h)[None, None, :, None]
    if n_sel > 0:
        kb = kp.reshape(b, nb, MOBA_BLOCK, h, dh)
        kmean = jnp.mean(kb.astype(jnp.float32), axis=2)
        gate = jnp.einsum('bthd,bnhd->bthn', q.astype(jnp.float32), kmean)
        past = jnp.arange(nb)[None, :] < qblk[:, None]
        gate = jnp.where(past[None, :, None, :], gate, -jnp.inf)
        _, sel = lax.top_k(gate, n_sel)
        sel_ok = sel < qblk[None, :, None, None]
        kbh = kb.transpose(0, 3, 1, 2, 4)
        vbh = vp.reshape(b, nb, MOBA_BLOCK, h, dh).transpose(0, 3, 1, 2, 4)

    def chunk(c):
        t0 = c * Q_CHUNK
        qc = lax.dynamic_slice_in_dim(q, t0, Q_CHUNK, axis=1)
        b0 = (t0 // MOBA_BLOCK) * MOBA_BLOCK
        k_own = lax.dynamic_slice_in_dim(kp, b0, MOBA_BLOCK, axis=1)
        v_own = lax.dynamic_slice_in_dim(vp, b0, MOBA_BLOCK, axis=1)
        own_mask = (b0 + jnp.arange(MOBA_BLOCK))[None, :] <= (t0 + jnp.arange(Q_CHUNK))[:, None]
        if n_sel > 0:
            idx = lax.dynamic_slice_in_dim(sel, t0, Q_CHUNK, axis=1)
            ok = lax.dynamic_slice_in_dim(sel_ok, t0, Q_CHUNK, axis=1)
            return moba_attend(qc, k_own, v_own, own_mask, kbh[bi, hi, idx], vbh[bi, hi, idx], ok)
        return moba_attend(qc, k_own, v_own, own_mask, None, None, None)

    out = lax.map(chunk, jnp.arange(t // Q_CHUNK))
    return out.transpose(1, 0, 2, 3, 4).reshape(b, t, h, dh)

def moba_sample(q, k, v, cache_k, cache_v, page_table):
    bd, s, h, dh = q.shape
    ppb = MOBA_BLOCK // PAGE_SIZE
    n_full = PAST_LEN // MOBA_BLOCK
    rem = PAST_LEN - n_full * MOBA_BLOCK
    n_sel = min(MOBA_TOPK, n_full)
    if rem > 0:
        pt_rem = page_table[:, n_full * ppb:]
        k_own = jnp.concatenate([cache_k[pt_rem].reshape(bd, rem, h, dh).astype(k.dtype), k], axis=1)
        v_own = jnp.concatenate([cache_v[pt_rem].reshape(bd, rem, h, dh).astype(v.dtype), v], axis=1)
    else:
        k_own, v_own = k, v
    own_mask = jnp.arange(rem + s)[None, :] <= (rem + jnp.arange(s))[:, None]
    if n_sel == 0:
        return moba_attend(q, k_own, v_own, own_mask, None, None, None)
    pt_full = page_table[:, :n_full * ppb]
    kmean = jnp.mean(cache_k[pt_full].reshape(bd, n_full, MOBA_BLOCK, h, dh).astype(jnp.float32), axis=2)
    gate = jnp.einsum('bshd,bnhd->bshn', q.astype(jnp.float32), kmean)
    _, sel = lax.top_k(gate, n_sel)
    logical = sel[..., None] * ppb + jnp.arange(ppb)
    phys = page_table[jnp.arange(bd)[:, None, None, None, None], logical]
    hi = jnp.arange(h)[None, None, :, None, None]
    k_sel = cache_k[phys, :, hi, :].reshape(bd, s, h, n_sel, MOBA_BLOCK, dh).astype(k.dtype)
    v_sel = cache_v[phys, :, hi, :].reshape(bd, s, h, n_sel, MOBA_BLOCK, dh).astype(v.dtype)
    ok = jnp.ones((bd, s, h, n_sel), dtype=bool)
    return moba_attend(q, k_own, v_own, own_mask, k_sel, v_sel, ok)

def peer_ffn(x, w_pq, sub_keys, expert_u, expert_v):
    n, d = x.shape
    q = (x @ w_pq).reshape(n, PEER_HEADS, 2, PEER_DQ // 2).astype(jnp.float32)
    s = jnp.einsum('nhpd,pkd->nhpk', q, sub_keys.astype(jnp.float32))
    sv, si = lax.top_k(s, PEER_TOPK)
    comb = (sv[:, :, 0, :, None] + sv[:, :, 1, None, :]).reshape(n, PEER_HEADS, PEER_TOPK * PEER_TOPK)
    cs, ci = lax.top_k(comb, PEER_TOPK)
    e1 = jnp.take_along_axis(si[:, :, 0], ci // PEER_TOPK, axis=-1)
    e2 = jnp.take_along_axis(si[:, :, 1], ci % PEER_TOPK, axis=-1)
    idx = e1 * PEER_NKEYS + e2
    g = jax.nn.softmax(cs, axis=-1)
    c = min(PEER_CHUNK, n)
    n_pad = -(-n // c) * c
    nc = n_pad // c
    xp = jnp.pad(x, ((0, n_pad - n), (0, 0))).reshape(nc, c, d)
    ip = jnp.pad(idx, ((0, n_pad - n), (0, 0), (0, 0))).reshape(nc, c, PEER_HEADS, PEER_TOPK)
    gp = jnp.pad(g, ((0, n_pad - n), (0, 0), (0, 0))).reshape(nc, c, PEER_HEADS, PEER_TOPK)

    def body(args):
        xc, ic, gc = args
        act = jax.nn.gelu(jnp.einsum('cd,chkd->chk', xc, expert_u[ic]).astype(jnp.float32), approximate=False)
        return jnp.einsum('chk,chkd->cd', (gc * act).astype(x.dtype), expert_v[ic])

    out = lax.map(body, (xp, ip, gp))
    return out.reshape(n_pad, d)[:n]

def merge_and_ffn(x, r_out, a_out, w_out, norm_ffn, w_pq, sub_keys, expert_u, expert_v):
    b, t, d = x.shape
    h = x + jnp.concatenate([r_out, a_out.reshape(b, t, W_ATT)], axis=-1) @ w_out
    f = peer_ffn(rms_norm(h, norm_ffn).reshape(b * t, d), w_pq, sub_keys, expert_u, expert_v)
    return h + f.reshape(b, t, d)

def setup_inputs(seed: int = 0) -> dict:
    key = jax.random.key(seed)
    ks = jax.random.split(key, 32)
    f32 = jnp.float32
    n_pages = PAST_LEN // PAGE_SIZE
    n_used = DEC_BATCH * n_pages
    n_pool = n_used + n_used // 4
    L = DEPTH
    nrm = lambda k, shape, sc: jax.random.normal(k, shape, f32) * sc
    return {
        'x_prompt': nrm(ks[0], (BATCH, SEQ, D_MODEL), 1.0),
        'x_sample': nrm(ks[1], (DEC_BATCH, DEC_SEQ, D_MODEL), 1.0),
        'cache_k': nrm(ks[2], (L, n_pool, PAGE_SIZE, H_ATT, D_HEAD), 1.0),
        'cache_v': nrm(ks[3], (L, n_pool, PAGE_SIZE, H_ATT, D_HEAD), 1.0),
        'page_table': jax.random.permutation(ks[4], n_pool)[:n_used].reshape(DEC_BATCH, n_pages).astype(jnp.int32),
        'state_wkv': nrm(ks[5], (L, DEC_BATCH, H_RWKV, D_HEAD, D_HEAD), 0.3),
        'state_shift': nrm(ks[6], (L, DEC_BATCH, W_RWKV_IN), 1.0),
        'norm_mix': 1.0 + nrm(ks[7], (L, D_MODEL), 0.02),
        'w_in': nrm(ks[8], (L, D_MODEL, W_IN), D_MODEL ** -0.5),
        'mu_shift': jax.random.uniform(ks[9], (L, W_RWKV_IN), f32),
        'w0': jax.random.uniform(ks[10], (L, W_RWKV), f32, minval=-5.0, maxval=0.0),
        'w_decay_up': nrm(ks[11], (L, D_DECAY_LORA, W_RWKV), 0.1),
        'a0': nrm(ks[12], (L, W_RWKV), 0.1),
        'w_aaa_up': nrm(ks[13], (L, D_AAA_LORA, W_RWKV), 0.1),
        'w_gate_up': nrm(ks[14], (L, D_GATE_LORA, W_RWKV), D_GATE_LORA ** -0.5),
        'k_k': 0.85 + nrm(ks[15], (L, W_RWKV), 0.02),
        'k_a': 1.0 + nrm(ks[16], (L, W_RWKV), 0.02),
        'r_k': nrm(ks[17], (L, H_RWKV, D_HEAD), 0.1),
        'gn_gain': 1.0 + nrm(ks[18], (L, W_RWKV), 0.02),
        'gn_bias': nrm(ks[19], (L, W_RWKV), 0.02),
        'w_out': nrm(ks[20], (L, W_RWKV + W_ATT, D_MODEL), (W_RWKV + W_ATT) ** -0.5),
        'norm_ffn': 1.0 + nrm(ks[21], (L, D_MODEL), 0.02),
        'w_pq': nrm(ks[22], (L, D_MODEL, PEER_HEADS * PEER_DQ), D_MODEL ** -0.5),
        'peer_sub_keys': nrm(ks[23], (L, 2, PEER_NKEYS, PEER_DQ // 2), (PEER_DQ // 2) ** -0.5),
        'expert_u': nrm(ks[24], (L, PEER_EXPERTS, D_MODEL), D_MODEL ** -0.5),
        'expert_v': nrm(ks[25], (L, PEER_EXPERTS, D_MODEL), 0.3),
        'norm_final': 1.0 + nrm(ks[26], (D_MODEL,), 0.02),
    }

def reference(x_prompt, x_sample, cache_k, cache_v, page_table, state_wkv, state_shift, norm_mix, w_in, mu_shift, w0, w_decay_up, a0, w_aaa_up, w_gate_up, k_k, k_a, r_k, gn_gain, gn_bias, w_out, norm_ffn, w_pq, peer_sub_keys, expert_u, expert_v, norm_final):
    pos_p = jnp.arange(x_prompt.shape[1], dtype=jnp.int32)
    pos_s = PAST_LEN + jnp.arange(x_sample.shape[1], dtype=jnp.int32)
    xp, xs = x_prompt, x_sample
    kp_l, vp_l, sp_l, hp_l = [], [], [], []
    ks_l, vs_l, ss_l, hs_l = [], [], [], []
    for l in range(DEPTH):
        rw = (mu_shift[l], w0[l], w_decay_up[l], a0[l], w_aaa_up[l], w_gate_up[l], k_k[l], k_a[l], r_k[l], gn_gain[l], gn_bias[l])
        ffn = (w_out[l], norm_ffn[l], w_pq[l], peer_sub_keys[l], expert_u[l], expert_v[l])
        pr, q, k, v = project(xp, norm_mix[l], w_in[l], pos_p)
        bsz = xp.shape[0]
        r_out, s_new, sh_new = rwkv_group(pr, jnp.zeros((bsz, W_RWKV_IN), pr.dtype), jnp.zeros((bsz, H_RWKV, D_HEAD, D_HEAD), jnp.float32), *rw)
        a_out = moba_prompt(q, k, v)
        xp = merge_and_ffn(xp, r_out, a_out, *ffn)
        kp_l.append(k); vp_l.append(v); sp_l.append(s_new.astype(state_wkv.dtype)); hp_l.append(sh_new.astype(state_shift.dtype))
        pr, q, k, v = project(xs, norm_mix[l], w_in[l], pos_s)
        r_out, s_new, sh_new = rwkv_group(pr, state_shift[l], state_wkv[l], *rw)
        a_out = moba_sample(q, k, v, cache_k[l], cache_v[l], page_table)
        xs = merge_and_ffn(xs, r_out, a_out, *ffn)
        ks_l.append(k); vs_l.append(v); ss_l.append(s_new.astype(state_wkv.dtype)); hs_l.append(sh_new.astype(state_shift.dtype))
    y_prompt = rms_norm(xp, norm_final)
    y_sample = rms_norm(xs, norm_final)
    return (y_prompt, y_sample, jnp.stack(kp_l), jnp.stack(vp_l), jnp.stack(sp_l), jnp.stack(hp_l), jnp.stack(ks_l), jnp.stack(vs_l), jnp.stack(ss_l), jnp.stack(hs_l))


_drawn_inputs = setup_inputs


def setup_inputs(seed=0):
    import zlib

    import numpy as np

    out = dict(_drawn_inputs(seed))
    spreads = {}
    factors = {'k_k': 59.433,
     'k_a': 2.67,
     'gn_gain': 9.311,
     'gn_bias': 18.236,
     'norm_final': 21.665,
     'norm_ffn': 11.342,
     'cache_k': 3.472,
     'cache_v': 3.432}
    for name, (base, spread) in spreads.items():
        noise = np.random.default_rng([zlib.crc32(name.encode()), seed]).standard_normal(out[name].shape)
        drawn = base * np.exp(spread * noise) if base else spread * noise
        out[name] = __import__('jax').numpy.asarray(drawn.astype(out[name].dtype))
    for name, factor in factors.items():
        out[name] = (out[name] * factor).astype(out[name].dtype)
    return out
```

```python
import concourse.bass as bass
from concourse import mybir
from contextlib import ExitStack
import numpy as np

F32 = mybir.dt.float32
I32 = mybir.dt.int32
U32 = mybir.dt.uint32
ALU = mybir.AluOpType
ACT = mybir.ActivationFunctionType
AX = mybir.AxisListType.X

P = 128
D_MODEL, SEQ, NB, PAST, PAGE = 1024, 256, 8, 2048, 128
DH, NH = 64, 8
W = NH * DH
W_RWKV_IN = 3 * W + 256
W_IN = W_RWKV_IN + 3 * W
NPAGE = PAST // PAGE
N_POOL = NB * NPAGE * 5 // 4
T = SEQ + NB
KC = D_MODEL // P
NF = W_RWKV_IN // P
NP4 = W // P
CHUNK = 64
NCH = SEQ // CHUNK
SCALE = DH ** -0.5
GN_EPS, NORM_EPS = 64e-5, 1e-6
PEER_H, NKEYS, TOPK = 8, 128, 16
NJ = PEER_H * TOPK
BIG = 1.0e30
EXPM05 = float(np.exp(np.float64(-0.5)))

C_MATS = ["ident", "blk", "strictU", "inclU", "lvl0L", "lvl0U",
          "lvl1U", "lvl2U", "lvl3U", "lvl4U", "lvl5U", "causal"]
C_OFF = {n: i * P for i, n in enumerate(C_MATS)}
_o = len(C_MATS) * P
for _n, _w in (("rope", 2 * 16), ("rope_s", 16), ("iota16", 16), ("lower8", 64), ("scan", SEQ),
               ("own8", NB), ("eps", 1), ("dup64", DH)):
    C_OFF[_n] = _o
    _o += _w
C_COLS = _o
PRM_W = [("mu", NF), ("w0", NP4), ("a0", NP4), ("k_k", NP4), ("k_a", NP4), ("r_k", NP4),
         ("gn_g", NP4), ("gn_b", NP4), ("norm_mix", KC)]
PRM_OFF, _o = {}, 0
for _n, _w in PRM_W:
    PRM_OFF[_n] = _o
    _o += _w
PRM_COLS = _o


def constants():
    c = np.zeros((P, C_COLS), np.float32)
    i, j = np.arange(P)[:, None], np.arange(P)[None, :]
    same = i // CHUNK == j // CHUNK

    def put(name, m):
        c[:m.shape[0], C_OFF[name]:C_OFF[name] + m.shape[1]] = m

    put("ident", i == j)
    put("blk", i // DH == j // DH)
    put("strictU", same & (i < j))
    put("inclU", same & (i <= j))
    for lvl in range(6):
        up = (i >> (lvl + 1) == j >> (lvl + 1)) & ((i >> lvl) % 2 == 0) & ((j >> lvl) % 2 == 1)
        put(f"lvl{lvl}U", up)
        if lvl == 0:
            put("lvl0L", up.T)
    put("causal", np.where(i >= j, 0.0, -BIG))
    inv = (1.0 / (np.float32(500000.0) ** (np.arange(8, dtype=np.float32) * np.float32(2.0) / np.float32(16)))).astype(np.float32)
    ang = (np.arange(SEQ, dtype=np.float32)[:, None] * inv[None]).astype(np.float32)
    rope = np.concatenate([np.cos(ang), np.sin(ang)], 1).astype(np.float32).reshape(2, P, 16)
    put("rope", rope.transpose(1, 0, 2).reshape(P, 32))
    ang = (np.float32(PAST) * inv).astype(np.float32)
    put("rope_s", np.tile(np.concatenate([np.cos(ang), np.sin(ang)])[None], (P, 1)))
    put("iota16", np.tile(np.arange(16)[None], (P, 1)))
    put("lower8", np.tile((np.arange(8)[None, :] < np.arange(8)[:, None]).reshape(1, 64), (P, 1)))
    put("scan", np.tile((np.arange(SEQ) % CHUNK != 0)[None], (P, 1)))
    put("eps", np.full((P, 1), NORM_EPS))
    put("dup64", i % DH == np.arange(DH)[None])
    put("own8", np.arange(64)[:, None] // 8 == np.arange(8)[None])
    return c


def constants8():
    return (np.arange(8)[:, None] == np.arange(NB * P)[None] // P).astype(np.float32)



W_LOADS = [("w_in", 3 * W)] + [("w_in", 256 * n) for n in range(6)] + \
    [("w_in", W_RWKV_IN + 256 * n) for n in range(6)]
QKV_LOAD = 7
H_LOAD = [13, 25]
Q_LOAD = [17, 29]
for _ in range(2):
    W_LOADS += [("w_out", 256 * n) for n in range(4)] + [("w_pq", 256 * n) for n in range(8)]
W_SLOT = [n % 6 for n in range(25)] + [4 + n % 2 for n in range(12)]


def last_use(n):
    if n == 0:
        return ("pT", 13)
    if n < QKV_LOAD:
        return ("pT", 2 * (n - 1) + 1)
    if n < H_LOAD[0]:
        return ("qkv", (n - QKV_LOAD) // 2, 2)
    for g, t in ((0, 0), (1, 2)):
        if n < Q_LOAD[g]:
            return ("h", t, (n - H_LOAD[g]) // 2)
        if n < Q_LOAD[g] + 8:
            return ("qT", g, n - Q_LOAD[g])


def schedule():
    o = []
    cache = [0]

    def pages(n):
        for _ in range(n):
            o.append(("cache", cache[0]))
            cache[0] += 1

    def rwkv(tt, fill):
        o.extend([("nat", tt, a) for a in range(4)])
        o.extend([("A", tt, hg, k) for hg in range(2) for k in range(3)])
        o.append(("G", tt))
        for lvl in range(1, 6):
            o.extend([("P", tt, lvl, hg) for hg in range(2)])
            o.extend(fill[lvl - 1])
            o.extend([(k, tt, lvl, hg) for hg in range(2) for k in ("XP", "XPT")])
        o.extend([("U0", tt), ("TZ", tt, 0), ("TZ", tt, 1)])
        o.extend([("A", tt, hg, k) for hg in range(2) for k in (3, 4)])
        for c in (2 * tt, 2 * tt + 1):
            o.extend([("U", c), ("ys", c), ("dS", c)])
        o.extend([("yi", tt, 0), ("yi", tt, 1)])

    o += [("xT", t, h) for t in range(3) for h in range(2)]
    o += [("pT", f) for f in [12, 13] + list(range(12))]
    o += [("dec", p) for p in range(4)] + [("aaa", p) for p in range(4)] + [("gate", p) for p in range(4)]
    o += [("qkv", 0, 0)] + [("ss", p) for p in range(4)] + [("qkv", 1, 0), ("qkv", 2, 0)]
    o += [("bon", p) for p in range(4)]
    o += [("qkT", 0, 0), ("qkT", 0, 1)]
    rwkv(0, [[("S", 0), ("qkv", 0, 1)], [("PT", 0), ("qkv", 0, 2)], [("PV", 0), ("S", 1), ("qkv", 1, 1)],
             [("PT", 1), ("qkv", 1, 2)], [("PV", 1), ("qkv", 2, 1)]])
    o += [("qkv", 2, 2)]
    o += [("mean", 0), ("var", 0), ("h", 0, 0), ("h", 0, 1)]
    o += [("qkT", 1, 0), ("qkT", 1, 1), ("qkT", 2, 0), ("qkT", 2, 1)]
    o += [("xfT", 0, 0), ("xfT", 0, 1)]
    o += [("qT", 0, j) for j in range(8)]
    o += [("own",)]
    pages(1)
    o += [("sc", 0, 0), ("sc", 0, 1)]
    pages(3)
    o += [("sc", 0, 2), ("sc", 0, 3)]
    pages(8)
    for u in range(2, 6):
        o += [("S", u), ("PT", u), ("PV", u)]
        pages(2)
    for k in range(3):
        o += [("sE", k, i) for i in range(4)]
        pages(4)
    assert cache[0] == 32
    rwkv(1, [[], [("PTs", 0), ("PTs", 1), ("poD",)], [], [], []])
    at = o.index(("P", 1, 3, 0))
    tail = o[at:]
    del o[at:]
    for n, x in enumerate(tail):
        o.append(x)
        if n in (3, 5, 9, 11, 15, 17, 20, 22, 24, 26):
            pages(1)
    o += [("Sout",), ("mean", 1), ("var", 1)]
    pages(64 - cache[0])
    o += [("OT",), ("mean", 2), ("var", 2)]
    o += [("h", t, hf) for hf in range(2) for t in (1, 2)]
    o += [("xfT", t, h) for t in (1, 2) for h in range(2)]
    o += [("qT", 1, j) for j in range(8)]
    o += [("sc", t, g) for t in (1, 2) for g in range(4)]
    o += [("jT",)]
    for b in range(NB):
        o += [("xb", b, 0), ("xb", b, 1)]
    return o


def bc(ap, *shape):
    return ap.broadcast_to(list(shape))


class Chain:

    def __init__(self, eng, sem):
        self.eng, self.sem, self.base, self.n = eng, sem, 0, 0

    def inc(self, ins):
        ins.then_inc(self.sem, 1)
        self.n += 1

    def wait(self):
        self.eng.wait_ge(self.sem, self.base + self.n)

    def link(self, ins):
        self.inc(ins)
        self.wait()


def step_kernel(nc, A, O):
    ctx = ExitStack()
    with ctx:
        def sb(name, shape, dt=F32):
            return ctx.enter_context(nc.sbuf_tensor(name, shape, dt))

        def sem(name):
            return ctx.enter_context(nc.semaphore(name))

        const = sb("const", [P, C_COLS])

        def C(name, w=P, rows=P):
            return const[0:rows, C_OFF[name]:C_OFF[name] + w]

        ident = C("ident")
        prm = sb("prm", [P, PRM_COLS])

        def prmv(name):
            return prm[:, PRM_OFF[name]:PRM_OFF[name] + dict(PRM_W)[name]]

        def grid(region, off, *dims):
            v = region[:, off:off + int(np.prod(dims))]
            names = [chr(97 + i) for i in range(len(dims))]
            if len(dims) == 1:
                return v
            return v.rearrange(f"p ({' '.join(names)}) -> p {' '.join(names)}", **dict(zip(names[1:], dims[1:])))

        RS = 8
        ring = sb("ring", [P, 12, 1024])
        wslot = [ring[:, 2 * s:2 * s + 2, :].rearrange("p a b -> p (a b)").rearrange("p (c n) -> p c n", c=KC)
                 for s in range(6)]
        cache = sb("cache", [P, 4, 512])
        xT = sb("xT", [P, KC, T])
        qkT = xT
        GN = P + NB
        tmpY = sb("tmpY", [P, 512])
        tmpY4 = grid(tmpY, 0, 4, P)
        amr = sb("amr", [P, 6144])
        MT, X, XT, MTl, AzkT, PM = [grid(amr, 1024 * k, NH, P) for k in range(6)]
        ArbT, ArkT = MT, MTl
        r16 = grid(amr, 0, 4, 16, 8)
        Ss, St = grid(amr, 0, 4, NB, DH), grid(amr, 2048, 4, NB, DH)
        qT = amr[:, 0:16 * GN]
        comb = grid(amr, 0, 8, 256)
        oh = grid(amr, 0, NJ, 16)
        RO = 16 * GN
        sv = grid(amr, RO, 16, 16)
        si_u = grid(amr, RO + 256, 16, 16).bitcast(U32)
        sif = grid(amr, RO + 512, 16, 16)
        cs = grid(amr, RO + 768, 8, 16)
        ehi, elo, e1, e2, idxf = [amr[:, RO + 896 + 128 * k:RO + 1024 + 128 * k] for k in range(5)]
        ci_u, hi_u = [amr[:, RO + 1536 + 128 * k:RO + 1664 + 128 * k].bitcast(U32) for k in range(2)]
        mx8 = amr[:, RO + 1792:RO + 1800]
        work = grid(amr, RO + 1800, 4, 256)
        ps = sb("ps", [P, 12, T])
        F_a, F_g, F_kk, F_C, F_bonus = [sb(n, [P, NP4, T]) for n in ("F_a", "F_g", "F_kk", "F_C", "F_bonus")]
        F_y = F_C
        hx = sb("hx", [P, 6144])
        pT = grid(hx, 0, NF, T + 1)
        lx = grid(hx, NF * (T + 1), 2, T)
        F_logw = grid(hx, NF * (T + 1) + 2 * T, NP4, T)
        F_E = grid(hx, 0, NP4, T)
        hb = grid(hx, 0, 3, D_MODEL)
        xf = grid(hx, 3072, 3, D_MODEL)
        Qz = grid(hx, 4096, 4, NB, 64)
        PTs = grid(hx, 4096, NPAGE, 64)
        sc_s = hx[:, 1024:3072]
        stage = sb("stage", [P, 3, 2 * W])
        xn = stage[:, :, :]
        vN = sb("vN", [P, 3, W])
        Un, Gn = sb("Un", [P, W]), sb("Gn", [P, W])
        TZT, SBD = sb("TZT", [P, NP4, P]), sb("SBD", [P, NP4, P])
        att_s, att_p, att_t = grid(Un, 0, 4, P), TZT[:], tmpY4
        shout = TZT[:, :, :].rearrange("p a b -> p (a b)")[:, 0:NF * (NB + 1)].rearrange("p (a b) -> p a b", a=NF)
        cat = sb("cat", [P, 2 * NP4, T])
        loraW = cat[:, :, :].rearrange("p a b -> p (a b)")[:, 0:2 * W]
        nat = sb("nat", [P, 4, W])
        xfT = nat[:, :, :].rearrange("p a b -> p (a b)")
        gain = sb("gain", [P, D_MODEL])
        sel8 = ps[0:NB, 0:4, :].rearrange("p a b -> p (a b)")[:, 0:NB * P]
        subk = sb("subk", [P, 2, P])
        pg = sb("pg", [1, NB * NPAGE], I32)
        sw, WC = sb("sw", [P, NP4, NB]), sb("WC", [P, NP4, NCH])
        g64, g64b = sb("g64", [64, 40]), sb("g64b", [64, 64])
        tie64 = Un[0:64, 0:64]
        small = sb("small", [NB, 64])
        st4 = sb("st4", [P, 16])
        idx = sb("idx", [P, 2, NJ], I32)
        idxh = sb("idxh", [P, 2, RS], I32)
        idxTs = sb("idxTs", [P, NB], I32)
        gate = sb("gate", [P, 2, NJ])
        gateS = F_g[0:NB, 0, 0:NJ]
        actv, wgt = sb("actv", [P, NJ]), sb("wgt", [P, NJ])
        act8, w8 = sb("act8", [P, 2 * RS]), sb("w8", [P, RS])
        gTs, actS = sb("gTs", [P, NB]), sb("actS", [P, NB])
        wSz = sb("wSz", [P, NB, NB])

        pS = ctx.enter_context(nc.psum_tensor("pS", [P, 2048], F32))
        pR = [ctx.enter_context(nc.psum_tensor(f"pR{i}", [P, 512], F32)) for i in range(4)]

        (const_in, prm_in, page_in, lora_in, gain_in, subk_in, sel8_in, shift_in, state_in) = [sem(n) for n in (
            "const_in", "prm_in", "page_in", "lora_in", "gain_in", "subk_in", "sel8_in", "shift_in", "state_in")]
        x_in = [sem(f"x_in{t}") for t in range(3)]
        x2_in = [sem(f"x2_in{t}") for t in range(3)]
        w_in_sem = [sem(f"w_in{s}") for s in range(6)]
        bank_filled = [sem(f"bank_filled{i}") for i in range(4)]
        bank_emptied = [sem(f"bank_emptied{i}") for i in range(4)]
        dve_step, act_step = sem("dve_step"), sem("act_step")
        (xsq, xnorm, roped, q_spread, att_masked, att_exp, att_norm) = [sem(n) for n in (
            "xsq", "xnorm", "roped", "q_spread", "att_masked", "att_exp", "att_norm")]
        (shifted, lora_act, kk_sq, kk_norm, rk_done, cum_ready, exp1, exp2, tilde) = [sem(n) for n in (
            "shifted", "lora_act", "kk_sq", "kk_norm", "rk_done", "cum_ready", "exp1", "exp2", "tilde")]
        (lvl_mask, x_init, state_ready, ysq_ready, gn_var, gn_std) = [sem(n) for n in (
            "lvl_mask", "x_init", "state_ready", "ysq_ready", "gn_var", "gn_std")]
        y_done = [sem(f"y_done{t}") for t in range(3)]
        cat_ready = sem("cat_ready")
        cache_in = [sem(f"cache_in{i}") for i in range(4)]
        cache_used = sem("cache_used")
        s_max, s_exp, s_prob, o_done, o_copied = [sem(n) for n in ("s_max", "s_exp", "s_prob", "o_done", "o_copied")]
        sst_ready, sst_done = sem("sst_ready"), sem("sst_done")
        h_ready, h_sq, xf_ready = sem("h_ready"), sem("h_sq"), sem("xf_ready")
        routed, cs_ready, g_exp = sem("routed"), sem("cs_ready"), sem("g_exp")
        idx_moved, slot_open = sem("idx_moved"), sem("slot_open")
        gathered = [sem(f"gathered{i}") for i in range(RS)]
        row_used = [sem(f"row_used{i}") for i in range(RS)]
        u_done, gelu_done, w_ready = sem("u_done"), sem("gelu_done"), sem("w_ready")
        sT_ready, sv_done = sem("sT_ready"), sem("sv_done")
        acc_ready, y_sq, y_ready = sem("acc_ready"), sem("y_sq"), sem("y_ready")
        out_kv = [sem(f"out_kv{t}") for t in range(3)]
        out_shift, out_state, out_sstate, out_y = [sem(n) for n in ("out_shift", "out_state", "out_sstate", "out_y")]
        shift_out_ready, sout_copied = sem("shift_out_ready"), sem("sout_copied")

        order = schedule()
        jobs = [x for x in order if x[0] != "cache"]
        J = {name: n for n, name in enumerate(jobs)}
        assert len(J) == len(jobs)

        def bank(job):
            return pR[J[job] % 4]

        def bank4(job, n=P):
            return bank(job)[:, 0:4 * n].rearrange("p (a b) -> p a b", a=4)

        def filled(eng, job):
            eng.wait_ge(bank_filled[J[job] % 4], J[job] // 4 + 1)

        def evacuated(eng, job):
            eng.wait_ge(bank_emptied[J[job] % 4], J[job] // 4 + 1)

        def empties(ins, job):
            ins.then_inc(bank_emptied[J[job] % 4], 1)

        tok = [(0, P), (P, P), (SEQ, NB)]
        grp = [(0, P, (0,)), (P, GN, (1, 2))]

        def cols(t):
            return slice(tok[t][0], tok[t][0] + tok[t][1])

        def w_arrived(eng, n):
            eng.wait_ge(w_in_sem[W_SLOT[n]], 16 * W_SLOT[:n + 1].count(W_SLOT[n]))

        def unit(u):
            if u < 2:
                return [(2 * n + u, 0) for n in range(4)]
            return [(4 * ((u - 2) // 2) + 2 * (n // 2) + u % 2, n % 2) for n in range(4)]

        def xfTg(g):
            n = grp[g][1]
            return xfT[:, 0:KC * n].rearrange("p (c n) -> p c n", c=KC)

        def slot(h):
            return 4 * (h % 2) + h // 2

        def OmS(b):
            return stage[0:NH, b // 2, (b % 2) * W:(b % 2 + 1) * W] if b < 6 else sc_s[0:NH, (b - 6) * W:(b - 5) * W]

        Zs, Bs, Rs, Ks, Vs = F_kk, F_a, ps[:, 0:4, :], ps[:, 4:8, :], ps[:, 8:12, :]
        block = ctx.enter_context(nc.Block())
        tv, ta, tg = nc.vector, nc.scalar, nc.gpsimd

        @block.sync
        def _(sp):
            def load_w(n):
                name, c0 = W_LOADS[n]
                before = [m for m in range(n) if W_SLOT[m] == W_SLOT[n]]
                if before:
                    filled(sp, last_use(before[-1]))
                sp.dma_start(wslot[W_SLOT[n]], A[name].rearrange("(c p) n -> p c n", p=P)[:, :, c0:c0 + 256])\
                    .then_inc(w_in_sem[W_SLOT[n]], 16)

            def load_pages(n0, n1, src):
                def one(n, first):
                    for j in range(4):
                        if j % 2 == 0 and not first:
                            sp.wait_ge(cache_used, n * 2 + (j // 2 - 1))
                        k = sp.value_load(pg[0:1, bass.ds((n * 4 + j) if n0 < 32 else (n * 4 + (j - 128)), 1)],
                                          min_val=0, max_val=N_POOL - 1)
                        sp.dma_start(cache[:, j, :], src[bass.ds(k, 1)].rearrange("a p n -> p (a n)"))\
                            .then_inc(cache_in[j], 16)
                if n1 - n0 == 1:
                    one(n0, n0 == 0)
                else:
                    with sp.Fori(n0, n1) as n:
                        one(n, False)

            sp.dma_start(xn[:, 0, :], A["x_prompt"][0, 0:P, :]).then_inc(x_in[0], 16)
            sp.dma_start(const[:], A["const"]).then_inc(const_in, 16)
            sp.dma_start(prm[:], A["prm"]).then_inc(prm_in, 16)
            load_w(0)
            sp.dma_start(xn[:, 1, :], A["x_prompt"][0, P:2 * P, :]).then_inc(x_in[1], 16)
            sp.dma_start(xn[0:NB, 2, :], A["x_sample"]).then_inc(x_in[2], 16)
            load_w(1)
            sp.dma_start(Un[:, 0:NF * NB], A["shiftT"]).then_inc(shift_in, 16)
            load_w(2)
            sp.dma_start(loraW, A["lora"]).then_inc(lora_in, 16)
            for n in range(3, 6):
                load_w(n)
            sp.dma_start(pg[:], A["pages"]).then_inc(page_in, 16)
            sp.dma_start(subk[:], A["subkT"]).then_inc(subk_in, 16)
            sp.dma_start(gain[:], A["norm_ffn"].partition_broadcast(P)).then_inc(gain_in, 16)
            for n in range(6, QKV_LOAD + 6):
                load_w(n)
            sp.wait_ge(page_in, 16)
            load_pages(0, 1, A["cache_k"])

            def store_kv(t):
                n = tok[t][1]
                ko, vo = (O["k_prompt"][t * P:(t + 1) * P, :], O["v_prompt"][t * P:(t + 1) * P, :]) if t < 2 else \
                    (O["k_sample"], O["v_sample"])
                sp.wait_ge(roped, t + 1)
                sp.dma_start(ko, stage[0:n, t, W:2 * W]).then_inc(out_kv[t], 16)
                sp.dma_start(vo, vN[0:n, t, :]).then_inc(out_kv[t], 16)

            sp.wait_ge(shift_out_ready, 1)
            sp.dma_start(O["shiftT"], shout.rearrange("p a b -> p (a b)")).then_inc(out_shift, 16)
            store_kv(0)
            for n in range(H_LOAD[0], Q_LOAD[0]):
                load_w(n)
            for n in range(Q_LOAD[0], Q_LOAD[0] + 2):
                load_w(n)
            evacuated(sp, ("var", 0))
            sp.wait_ge(tilde, 1)
            sp.dma_start(hb[:, 0, :], A["x_prompt"][0, 0:P, :]).then_inc(x2_in[0], 16)
            for n in range(Q_LOAD[0] + 2, Q_LOAD[0] + 8):
                load_w(n)
            store_kv(1)
            store_kv(2)
            load_pages(1, 12, A["cache_k"])
            sp.wait_ge(routed, 1)
            sp.dma_start(Ss.rearrange("p a b v -> p (a b v)"), A["state_wkv"]).then_inc(state_in, 16)
            load_pages(12, 32, A["cache_k"])
            sp.wait_ge(sst_done, 1)
            sp.dma_start(O["wkv_sample"], Ss.rearrange("p a b v -> p (a b v)")).then_inc(out_sstate, 16)
            load_w(H_LOAD[1])
            load_w(H_LOAD[1] + 1)
            load_pages(32, 64, A["cache_v"])
            sp.wait_ge(sout_copied, 1)
            so = Gn[:, :].rearrange("p (a b) -> p a b", a=NP4)
            for par in range(2):
                sp.dma_start(O["wkv_prompt"].rearrange("(a r) v k -> r v a k", r=2)[par],
                             so[par * 64:par * 64 + 64, :, par * 64:par * 64 + 64]).then_inc(out_state, 16)
            sp.dma_start(sel8, A["const8"]).then_inc(sel8_in, 16)
            filled(sp, ("OT",))
            sp.dma_start(hb[:, 1, :], A["x_prompt"][0, P:2 * P, :]).then_inc(x2_in[1], 16)
            sp.dma_start(hb[0:NB, 2, :], A["x_sample"]).then_inc(x2_in[2], 16)
            for n in range(H_LOAD[1] + 2, Q_LOAD[1] + 8):
                load_w(n)
            sp.wait_ge(xf_ready, 3)
            sp.dma_start(gain[:], A["norm_final"].partition_broadcast(P)).then_inc(gain_in, 16)
            for t in range(2):
                sp.wait_ge(y_ready, t + 1)
                sp.dma_start(O["y_prompt"][t * P:(t + 1) * P, :], xf[:, t, :]).then_inc(out_y, 16)
            sp.wait_ge(y_ready, 3)
            sp.dma_start(O["y_sample"], xf[0:NB, 2, :]).then_inc(out_y, 16)
            for t in range(3):
                sp.wait_ge(out_kv[t], 32)
            sp.wait_ge(out_shift, 16)
            sp.wait_ge(out_state, 32)
            sp.wait_ge(out_sstate, 16)
            sp.wait_ge(out_y, 48)

        @block.tensor
        def _(pe):
            mm, tr = nc.tensor.matmul, nc.tensor.transpose

            def begin(job):
                n = J[job]
                if n >= 4:
                    pe.wait_ge(bank_emptied[n % 4], n // 4)
                return pR[n % 4]

            def end(job, ins):
                ins.then_inc(bank_filled[J[job] % 4], 1)

            def j_xT(job, t, h):
                n = tok[t][1]
                pe.wait_ge(xnorm, t + 1)
                b = begin(job)
                for c in range(4):
                    i = tr(b[:, c * P:c * P + n], xn[0:n, t, (4 * h + c) * P:(4 * h + c + 1) * P], ident[0:n, 0:n])
                end(job, i)

            def j_pT(job, f):
                if f == 12:
                    for t in (1, 2):
                        for h in range(2):
                            evacuated(pe, ("xT", t, h))
                load, c0 = (0, (f - 12) * P) if f >= 12 else (1 + f // 2, (f % 2) * P)
                w_arrived(pe, load)
                b = begin(job)
                for c in range(KC):
                    i = mm(b[:, 0:T], wslot[W_SLOT[load]][:, c, c0:c0 + P], xT[:, c, :], start=(c == 0), stop=(c == KC - 1))
                end(job, i)

            def project(b, n, lhs, load0):
                for hf in range(2):
                    w_arrived(pe, load0 + hf)
                    for c in range(KC):
                        i = mm(b[0:n, hf * 256:(hf + 1) * 256], lhs(c), wslot[W_SLOT[load0 + hf]][:, c, :],
                               start=(c == 0), stop=(c == KC - 1))
                return i

            def j_qkv(job, part, t):
                t0, n = tok[t]
                b = begin(job)
                end(job, project(b, n, lambda c: xT[:, c, t0:t0 + n], QKV_LOAD + 2 * part))

            def j_qkT(job, t, w):
                n = tok[t][1]
                pe.wait_ge(roped, t + 1)
                b = begin(job)
                for p in range(4):
                    i = tr(b[:, p * P:p * P + n], stage[0:n, t, w * W + p * P:w * W + (p + 1) * P], ident[0:n, 0:n])
                end(job, i)

            def j_own(job):
                pe.wait_ge(q_spread, 1)
                evacuated(pe, ("qkT", 2, 1))
                b = begin(job)
                for s in range(NB):
                    for c in range(4):
                        i = mm(b[0:64, 0:1], Qz[:, c, s, :], qkT[:, 4 + c, SEQ + s:SEQ + s + 1],
                               start=(s == 0 and c == 0), stop=(s == NB - 1 and c == 3))
                end(job, i)

            def j_S(job, u):
                qt = 0 if u < 2 else 1
                evacuated(pe, ("qkT", qt, 0)); evacuated(pe, ("qkT", qt, 1))
                b = begin(job)
                for n, (h, kc) in enumerate(unit(u)):
                    r0 = (h % 2) * 64
                    i = mm(b[:, n * P:(n + 1) * P], qkT[r0:r0 + 64, h // 2, qt * P:(qt + 1) * P],
                           qkT[r0:r0 + 64, 4 + h // 2, kc * P:(kc + 1) * P], start=True, stop=True)
                end(job, i)

            def j_PT(job, u):
                pe.wait_ge(att_norm, u + 1)
                b = begin(job)
                for n in range(4):
                    i = tr(b[:, n * P:(n + 1) * P], att_p[:, n, :], ident)
                end(job, i)

            def j_PV(job, u):
                evacuated(pe, ("PT", u))
                evacuated(pe, ("qkv", 2, 0 if u < 2 else 1))
                b = begin(job)
                for n, (h, kc) in enumerate(unit(u)):
                    hh = n if u < 2 else n // 2
                    i = mm(b[:, hh * P:(hh + 1) * P], vN[:, kc, (h // 2) * P:(h // 2 + 1) * P],
                           att_t[:, n, :], start=(kc == 0), stop=(u < 2 or kc == 1))
                end(job, i)

            def unit_of_cache(n):
                b, g = (n % 32) // 4, n % 4
                if n == 0:
                    pe.wait_ge(q_spread, 1)
                if n == 32:
                    pe.wait_ge(s_prob, 1)
                    evacuated(pe, ("PTs", 0)); evacuated(pe, ("PTs", 1)); evacuated(pe, ("poD",))
                if n >= 32 and g == 0 and b >= 4:
                    pe.wait_ge(o_copied, b - 3)
                for hf in range(2):
                    pe.wait_ge(cache_in[2 * hf], 16 * (n + 1))
                    pe.wait_ge(cache_in[2 * hf + 1], 16 * (n + 1))
                    if n < 32:
                        rhs = cache[:, 2 * hf:2 * hf + 2, :].rearrange("p a (c t) -> p a c t", c=4)
                        for c in range(4):
                            i = mm(pS[0:64, g * 512 + hf * 256:g * 512 + (hf + 1) * 256], Qz[:, c, b, :], rhs[:, :, c, :],
                                   start=(n < 4 and hf == 0 and c == 0), stop=(b == NB - 1 and c == 3),
                                   skip_group_check=True)
                    else:
                        o = pS[0:NH, (b % 4) * 512:(b % 4 + 1) * 512]
                        for j in (2 * hf, 2 * hf + 1):
                            i = mm(o, PTs[:, 4 * g + j, 8 * b:8 * b + 8], cache[:, j, :],
                                   start=(g == 0 and j == 0), stop=False, skip_group_check=True)
                    i.then_inc(cache_used, 1)
                if n >= 32 and g == 3:
                    mm(o, small[:, 8 * b:8 * b + 8], vN[0:NB, 2, :], start=False, stop=True,
                       skip_group_check=True).then_inc(o_done, 1)

            def j_lora(job, p):
                rows, c0, rhs = {"dec": (slice(0, 64), 0, lx[0:64, 0, :]), "aaa": (slice(64, P), 0, lx[64:P, 0, :]),
                                 "gate": (slice(0, P), W, lx[:, 1, :])}[job[0]]
                pe.wait_ge(lora_in, 16)
                pe.wait_ge(lora_act, 2)
                b = begin(job)
                end(job, mm(b[:, 0:T], loraW[rows, c0 + p * P:c0 + (p + 1) * P], rhs, start=True, stop=True))

            def j_headsum(job, p):
                pe.wait_ge(kk_sq if job[0] == "ss" else rk_done, 1)
                b = begin(job)
                end(job, mm(b[:, 0:T], C("blk"), F_E[:, p, :], start=True, stop=True))

            def j_nat(job, tt, a):
                pe.wait_ge(tilde, 1)
                b = begin(job)
                for p in range(4):
                    i = tr(b[:, p * P:(p + 1) * P], (Vs, Zs, Bs, Ks)[a][:, p, cols(tt)], ident)
                end(job, i)

            def j_A(job, tt, hg, k):
                pe.wait_ge(tilde, 1)
                l, r = ((Bs, Zs), (Zs, Bs), (Ks, Zs), (Bs, Rs), (Ks, Rs))[k]
                r0 = hg * 64
                b = begin(job)
                for n in range(4):
                    i = mm(b[:, n * P:(n + 1) * P], l[r0:r0 + 64, n, cols(tt)], r[r0:r0 + 64, n, cols(tt)],
                           start=True, stop=True)
                end(job, i)

            def j_P(job, tt, lvl, hg):
                pe.wait_ge(lvl_mask, 10 * tt + 2 * (lvl - 1) + hg + 1)
                pe.wait_ge(x_init, 2 * tt + hg + 1)
                if lvl > 1:
                    evacuated(pe, ("XP", tt, lvl - 1, hg))
                b = begin(job)
                for n in range(4):
                    h = 4 * hg + n
                    i = mm(b[:, n * P:(n + 1) * P], MTl[:, h, :], X[:, h, :], start=True, stop=True)
                end(job, i)

            def j_XP(job, tt, lvl, hg):
                evacuated(pe, ("P", tt, lvl, hg))
                if lvl > 1:
                    evacuated(pe, ("XPT", tt, lvl - 1, hg))
                b = begin(job)
                for n in range(4):
                    h = 4 * hg + n
                    l, r = (XT[:, h, :], PM[:, h, :]) if job[0] == "XP" else (PM[:, h, :], XT[:, h, :])
                    i = mm(b[:, n * P:(n + 1) * P], l, r, start=True, stop=True)
                end(job, i)

            def j_G(job, tt):
                evacuated(pe, ("nat", tt, 0))
                evacuated(pe, ("A", tt, 0, 2)); evacuated(pe, ("A", tt, 1, 2))
                b = begin(job)
                for h in range(NH):
                    i = mm(b[:, h * 64:h * 64 + 64], AzkT[:, slot(h), :], nat[:, 0, h * 64:h * 64 + 64], start=True, stop=True)
                end(job, i)

            def j_U0(job, tt):
                evacuated(pe, ("XPT", tt, 5, 0)); evacuated(pe, ("XPT", tt, 5, 1)); evacuated(pe, ("G", tt))
                b = begin(job)
                for h in range(NH):
                    i = mm(b[:, h * 64:h * 64 + 64], XT[:, slot(h), :], Gn[:, h * 64:h * 64 + 64], start=True, stop=True)
                end(job, i)

            def j_TZ(job, tt, hf):
                evacuated(pe, ("nat", tt, 1))
                b = begin(job)
                for n in range(4):
                    h = 4 * hf + n
                    i = mm(b[:, n * P:(n + 1) * P], nat[:, 1, (h // 2) * P:(h // 2 + 1) * P], XT[:, slot(h), :],
                           start=True, stop=True)
                end(job, i)

            def j_U(job, c):
                evacuated(pe, ("TZ", c // 2, 0)); evacuated(pe, ("TZ", c // 2, 1))
                pe.wait_ge(state_ready, c + 1)
                b = begin(job)
                for p in range(4):
                    i = mm(b[:, p * P:(p + 1) * P], TZT[:, p, :], SBD[:, p, :], start=True, stop=True)
                end(job, i)

            def j_ys(job, c):
                b = begin(job)
                for p in range(4):
                    i = mm(b[:, p * CHUNK:(p + 1) * CHUNK], SBD[:, p, :], Rs[:, p, c * CHUNK:(c + 1) * CHUNK],
                           start=True, stop=True)
                end(job, i)

            def j_dS(job, c):
                rows = slice((c % 2) * 64, (c % 2) * 64 + 64)
                evacuated(pe, ("U", c))
                evacuated(pe, ("nat", c // 2, 2)); evacuated(pe, ("nat", c // 2, 3))
                b = begin(job)
                for p in range(4):
                    pc = slice(p * P, (p + 1) * P)
                    mm(b[:, pc], nat[rows, 2, pc], Un[rows, pc], start=True, stop=False)
                    i = mm(b[:, pc], nat[rows, 3, pc], nat[rows, 0, pc], start=False, stop=True)
                end(job, i)

            def j_yi(job, tt, hf):
                for hg in range(2):
                    evacuated(pe, ("A", tt, hg, 3)); evacuated(pe, ("A", tt, hg, 4))
                b = begin(job)
                for n in range(4):
                    h = 4 * hf + n
                    pc = slice((h // 2) * P, (h // 2 + 1) * P)
                    mm(b[:, n * P:(n + 1) * P], Un[:, pc], ArbT[:, slot(h), :], start=True, stop=False)
                    i = mm(b[:, n * P:(n + 1) * P], nat[:, 0, pc], ArkT[:, slot(h), :], start=False, stop=True)
                end(job, i)

            def j_Sout(job):
                pe.wait_ge(state_ready, 5)
                b = begin(job)
                for p in range(4):
                    i = tr(b[:, p * P:(p + 1) * P], SBD[:, p, :], ident)
                end(job, i)

            def j_sE(job, k, i):
                pe.wait_ge(sst_ready, 4 * k + i + 1)
                b = begin(job)
                end(job, mm(b[:, :], C("blk"), St[:, i, :, :].rearrange("p a b -> p (a b)"), start=True, stop=True))

            def j_PTs(job, hf):
                pe.wait_ge(s_prob, 1)
                b = begin(job)
                for j in range(8):
                    i = tr(b[:, j * 64:(j + 1) * 64], sc_s[0:64, (8 * hf + j) * P:(8 * hf + j + 1) * P], ident[0:64, 0:64])
                end(job, i)

            def j_poD(job):
                b = begin(job)
                end(job, mm(b[0:NB, 0:64], C("own8", NB, 64), g64b[:, :], start=True, stop=True))

            def j_OT(job):
                pe.wait_ge(o_copied, NB)
                bk = begin(job)
                for b in range(NB):
                    for c in range(4):
                        o = (c * NB + b) * 2
                        i = mm(bk[:, o:o + 2], OmS(b)[:, c * P:(c + 1) * P], ident[0:NH, 2 * c:2 * c + 2],
                               start=True, stop=True)
                end(job, i)

            def j_stat(job, t):
                n = tok[t][1]
                if job[0] == "mean":
                    pe.wait_ge(y_done[t], 1)
                else:
                    pe.wait_ge(ysq_ready, t + 1)
                b = begin(job)
                for p in range(4):
                    src = F_y[:, p, cols(t)] if job[0] == "mean" else tmpY[:, p * n:(p + 1) * n]
                    i = mm(b[:, p * n:(p + 1) * n], C("blk"), src, start=True, stop=True)
                end(job, i)

            def j_h(job, t, hf):
                t0, n = tok[t]
                pe.wait_ge(cat_ready, t + 1)
                b = begin(job)
                end(job, project(b, n, lambda c: cat[:, c, t0:t0 + n], H_LOAD[min(t, 1)] + 2 * hf))

            def j_xfT(job, t, h):
                n = tok[t][1]
                pe.wait_ge(xf_ready, t + 1)
                b = begin(job)
                for c in range(4):
                    i = tr(b[:, c * P:c * P + n], xf[0:n, t, (4 * h + c) * P:(4 * h + c + 1) * P], ident[0:n, 0:n])
                end(job, i)

            def j_qT(job, g, j):
                t0, n, ts = grp[g]
                if j == 0:
                    for t in ts:
                        evacuated(pe, ("xfT", t, 0)); evacuated(pe, ("xfT", t, 1))
                load = Q_LOAD[g] + j
                w_arrived(pe, load)
                b = begin(job)
                for k in range(2):
                    for c in range(KC):
                        i = mm(b[:, k * n:(k + 1) * n], wslot[W_SLOT[load]][:, c, k * P:(k + 1) * P], xfTg(g)[:, c, :],
                               start=(c == 0), stop=(c == KC - 1))
                end(job, i)

            def j_sc(job, t, q):
                g = min(t, 1)
                n, gn = tok[t][1], grp[g][1]
                o = tok[t][0] - grp[g][0]
                pe.wait_ge(subk_in, 16)
                evacuated(pe, ("qT", g, 2 * q)); evacuated(pe, ("qT", g, 2 * q + 1))
                b = begin(job)
                for k in range(4):
                    hp = 4 * q + k
                    i = mm(b[0:n, k * P:(k + 1) * P], qT[:, hp * gn + o:hp * gn + o + n], subk[:, hp % 2, :],
                           start=True, stop=True)
                end(job, i)

            def j_jT(job):
                pe.wait_ge(routed, 3)
                b = begin(job)
                tr(b[:, 0:NB], idxf[0:NB, :], ident[0:NB, 0:NB])
                end(job, tr(b[:, NB:2 * NB], gateS[:, :], ident[0:NB, 0:NB]))

            def j_xb(job, b, hf):
                pe.wait_ge(sel8_in, 16)
                bk = begin(job)
                end(job, mm(bk[:, :], sel8[:, b * P:(b + 1) * P], xf[0:NB, 2, hf * 512:(hf + 1) * 512],
                            start=True, stop=True))

            do = {"xT": j_xT, "pT": j_pT, "qkv": j_qkv, "qkT": j_qkT, "own": j_own, "S": j_S, "PT": j_PT, "PV": j_PV,
                  "dec": j_lora, "aaa": j_lora, "gate": j_lora, "ss": j_headsum, "bon": j_headsum, "nat": j_nat,
                  "A": j_A, "P": j_P, "XP": j_XP, "XPT": j_XP, "G": j_G, "U0": j_U0, "TZ": j_TZ, "U": j_U, "ys": j_ys,
                  "dS": j_dS, "yi": j_yi, "Sout": j_Sout, "sE": j_sE, "PTs": j_PTs, "poD": j_poD, "OT": j_OT,
                  "mean": j_stat, "var": j_stat, "h": j_h, "xfT": j_xfT, "qT": j_qT, "sc": j_sc, "jT": j_jT, "xb": j_xb}
            pe.wait_ge(const_in, 16)
            for x in order:
                if x[0] == "cache":
                    unit_of_cache(x[1])
                else:
                    do[x[0]](x, *x[1:])
            pe.wait_ge(w_ready, 1)
            for b in range(NB):
                pe.wait_ge(gathered[b], 16 * 66)
                for hf in range(2):
                    i = mm(pS[0:NB, hf * 512:(hf + 1) * 512], wSz[:, b, :], ring[:, b, hf * 512:(hf + 1) * 512],
                           start=(b == 0), stop=(b == NB - 1), skip_group_check=True)
            i.then_inc(sv_done, 1)

        @block.scalar
        def _(act):
            ch = Chain(act, act_step)

            def rms(src, scratch, dst, done):
                n = src.shape[0]
                ch.link(ta.activation(scratch, src, ACT.Square, scale=D_MODEL ** -0.5, accum_out=dst))
                ta.activation(dst, dst, ACT.Sqrt, bias=C("eps", 1, n)).then_inc(done, 1)

            def copy(dst, src, job):
                filled(act, job)
                empties(ta.activation(dst, src, ACT.Copy), job)

            act.wait_ge(const_in, 16)
            for t, (t0, n) in enumerate(tok):
                act.wait_ge(x_in[t], 16)
                rms(xn[0:n, t, :], hx[0:n, 5120:6144], st4[0:n, t:t + 1], xsq)
            for x in order:
                k, a = x[0], x[1:]
                if x == ("dec", 0):
                    act.wait_ge(shifted, 1)
                    ta.activation(lx[0:64, 0, :], lx[0:64, 0, :], ACT.Tanh).then_inc(lora_act, 1)
                    ta.activation(lx[:, 1, :], lx[:, 1, :], ACT.Sigmoid).then_inc(lora_act, 1)
                if x == ("qkT", 0, 0):
                    act.wait_ge(cum_ready, 1)
                    ta.activation(WC[:, :, :], F_C[:, :, CHUNK - 1:SEQ:CHUNK], ACT.Exp)
                    ta.activation(sw[:, :, :], F_logw[:, :, SEQ:T], ACT.Exp)
                    ta.activation(F_E[:, :, 0:SEQ], F_E[:, :, 0:SEQ], ACT.Exp).then_inc(exp1, 1)
                    act.wait_ge(cum_ready, 2)
                    ta.activation(F_logw[:, :, 0:SEQ], F_C[:, :, 0:SEQ], ACT.Exp, scale=-1.0)
                    ta.activation(F_E[:, :, 0:SEQ], F_C[:, :, 0:SEQ], ACT.Exp).then_inc(exp2, 1)
                if k == "PT":
                    act.wait_ge(att_masked, a[0] + 1)
                    nh = 4 if a[0] < 2 else 2
                    flat = att_s.rearrange("p a b -> p (a b)")
                    w = 512 // nh
                    for n in range(nh):
                        i = ta.activation(flat[:, n * w:(n + 1) * w], flat[:, n * w:(n + 1) * w], ACT.Exp,
                                          bias=st4[:, 4 + n:5 + n], scale=SCALE, accum_out=st4[:, 8 + n:9 + n])
                    i.then_inc(att_exp, 1)
                if x == ("P", 1, 1, 0):
                    act.wait_ge(s_max, 1)
                    ta.activation(sc_s[0:64, :], sc_s[0:64, :], ACT.Exp, bias=g64[:, 33:34], scale=SCALE,
                                  accum_out=g64[:, 34:35])
                    ta.activation(g64[:, 35:36], g64[:, 32:33], ACT.Exp, bias=g64[:, 33:34], scale=SCALE).then_inc(s_exp, 1)
                if x == ("P", 1, 3, 0):
                    act.wait_ge(u_done, 1)
                    ta.activation(actv[:, :], actv[:, :], ACT.Gelu).then_inc(gelu_done, 1)
                if x == ("xfT", 0, 0):
                    act.wait_ge(h_ready, 1)
                    rms(hb[:, 0, :], xf[:, 0, :], st4[:, 0:1], h_sq)
                if x == ("xfT", 1, 0):
                    for t in (1, 2):
                        act.wait_ge(h_ready, t + 1)
                        rms(hb[0:tok[t][1], t, :], xf[0:tok[t][1], t, :], st4[0:tok[t][1], t:t + 1], h_sq)
                if k == "pT":
                    copy(pT[:, a[0], 1:T + 1], bank(x)[:, 0:T], x)
                elif k == "qkv":
                    n = tok[a[1]][1]
                    dst = stage[0:n, a[1], a[0] * W:(a[0] + 1) * W] if a[0] < 2 else vN[0:n, a[1], :]
                    copy(dst, bank(x)[0:n, :], x)
                elif k == "PT":
                    copy(att_t.rearrange("p a b -> p (a b)"), bank(x)[:, :], x)
                elif k in ("dec", "aaa"):
                    dst, bias = (F_logw, "w0") if k == "dec" else (F_a, "a0")
                    filled(act, x)
                    empties(ta.activation(dst[:, a[0], :], bank(x)[:, 0:T], ACT.Sigmoid,
                                          bias=prmv(bias)[:, a[0]:a[0] + 1]), x)
                elif k == "gate":
                    copy(F_g[:, a[0], :], bank(x)[:, 0:T], x)
                elif k == "ss" and a[0] == 3:
                    for p in range(4):
                        evacuated(act, ("ss", p))
                    ta.activation(F_C[:, :, :], F_C[:, :, :], ACT.Sqrt).then_inc(kk_norm, 1)
                elif k == "nat":
                    copy(nat[:, a[1], :], bank(x)[:, :], x)
                elif k == "P":
                    hg = a[2]
                    copy(PM[:, 4 * hg:4 * hg + 4, :].rearrange("p a b -> p (a b)"), bank(x)[:, :], x)
                elif k in ("G", "U0", "Sout"):
                    copy(Gn[:, :], bank(x)[:, :], x)
                    if k == "Sout":
                        evacuated(act, x)
                        act.sem_inc(sout_copied, 1)
                elif k == "TZ":
                    filled(act, x)
                    act.wait_ge(out_shift, 16)
                    bv = bank(x)[:, :].rearrange("p (a r t) -> p a r t", a=2, r=2)
                    hf = a[1]
                    ta.activation(TZT[0:64, 2 * hf:2 * hf + 2, :], bv[0:64, :, 0, :], ACT.Copy)
                    empties(ta.activation(TZT[64:128, 2 * hf:2 * hf + 2, :], bv[64:128, :, 1, :], ACT.Copy), x)
                elif k == "ys":
                    c = a[0]
                    copy(F_y[:, :, c * CHUNK:(c + 1) * CHUNK], bank4(x, CHUNK), x)
                elif k == "PTs":
                    copy(PTs[:, 8 * a[0]:8 * a[0] + 8, :].rearrange("p a b -> p (a b)"), bank(x)[:, :], x)
                elif k == "poD":
                    copy(small[:, :], bank(x)[0:NB, 0:64], x)
                elif k == "cache" and a[0] >= 32 and a[0] % 4 == 3:
                    b = (a[0] - 32) // 4
                    act.wait_ge(o_done, b + 1)
                    if b == 0:
                        for t in range(3):
                            act.wait_ge(out_kv[t], 32)
                    ta.activation(OmS(b), pS[0:NH, (b % 4) * 512:(b % 4 + 1) * 512], ACT.Copy).then_inc(o_copied, 1)
                elif k == "var":
                    act.wait_ge(gn_var, a[0] + 1)
                    n4 = 4 * tok[a[0]][1]
                    ta.activation(tmpY[:, 0:n4], tmpY[:, 0:n4], ACT.Sqrt).then_inc(gn_std, 1)
                elif k == "qT":
                    g, j = a
                    n = grp[g][1]
                    copy(qT[:, 2 * j * n:(2 * j + 2) * n], bank(x)[:, 0:2 * n], x)
                elif k == "sc" and a[1] == 3:
                    t = a[0]
                    if t == 2:
                        act.wait_ge(acc_ready, 1)
                        rms(hb[:, 0, :], xf[:, 0, :], st4[:, 12:13], y_sq)
                    g_ = gate[:, t, :] if t < 2 else gateS[:, :]
                    act.wait_ge(cs_ready, t + 1)
                    ta.activation(g_, g_, ACT.Exp).then_inc(g_exp, 1)
            act.wait_ge(u_done, 2)
            ta.activation(actv[:, :], actv[:, :], ACT.Gelu).then_inc(gelu_done, 1)
            act.wait_ge(acc_ready, 2)
            rms(hb[:, 1, :], xf[:, 1, :], st4[:, 12:13], y_sq)
            act.wait_ge(u_done, 3)
            ta.activation(actS[:], actS[:], ACT.Gelu).then_inc(gelu_done, 1)
            act.wait_ge(acc_ready, 3)
            rms(hb[0:NB, 2, :], xf[0:NB, 2, :], st4[0:NB, 12:13], y_sq)

        @block.gpsimd
        def _(pool):
            def masks(tt):
                for lvl in range(1, 6):
                    for hg in range(2):
                        hs = slice(4 * hg, 4 * hg + 4)
                        pool.wait_ge(x_init, 2 * tt + hg + 1)
                        if lvl > 1:
                            filled(pool, ("P", tt, lvl - 1, hg))
                        tg.tensor_tensor(MTl[:, hs, :], MT[:, hs, :],
                                         bc(C(f"lvl{lvl}U").unsqueeze(1), P, 4, P), ALU.mult).then_inc(lvl_mask, 1)

            def gathers(t, kind, i, q0, first):
                table = A["expert_u"] if kind == 0 else A["expert_v"]
                for par in range(2):
                    for s in range(RS):
                        if not (first and par == 0):
                            pool.wait_ge(row_used[s], i * 2 + (q0 + par))
                            pool.sem_inc(slot_open, 1)
                        if s == 0:
                            tg.tensor_copy(idxh[:, par, :], idx[:, t, bass.ds(i * 2 * RS + par * RS, RS)])\
                                .then_inc(idx_moved, 1)
                            pool.wait_ge(idx_moved, i * 2 + (q0 + par + 1))
                            pool.sem_inc(slot_open, 1)
                        tg.indirect_dma_start(ring[:, s, :], None, table,
                                              bass.IndirectOffsetOnAxis(ap=idxh[:, par, s:s + 1], axis=0))\
                            .then_inc(gathered[s], 16)

            pool.wait_ge(const_in, 16)
            masks(0)
            pool.wait_ge(routed, 1)
            filled(pool, ("qT", 0, 7))
            gathers(0, 0, 0, 0, True)
            with pool.Fori(1, PEER_H) as i:
                gathers(0, 0, i, 0, False)
            with pool.Fori(0, PEER_H) as i:
                gathers(0, 1, i, 16, False)
            for kind in range(2):
                q0 = 32 + 16 * kind
                if kind == 0:
                    pool.wait_ge(routed, 2)
                with pool.Fori(0, PEER_H) as i:
                    gathers(1, kind, i, q0, False)
            pool.wait_ge(sT_ready, 1)
            for kind, table in ((0, A["expert_u"]), (1, A["expert_v"])):
                for b in range(NB):
                    pool.wait_ge(row_used[b], 64 + kind)
                    tg.indirect_dma_start(ring[:, b, :], None, table,
                                          bass.IndirectOffsetOnAxis(ap=idxTs[:, b:b + 1], axis=0))\
                        .then_inc(gathered[b], 16)

        @block.vector
        def _(dve):
            ch = Chain(dve, dve_step)
            L = ch.link
            tt_, ts_, stt = tv.tensor_tensor, tv.tensor_scalar, tv.scalar_tensor_tensor

            def mask4(name):
                return bc(C(name).unsqueeze(1), P, 4, P)

            L(tv.memset(pT[:, :, 0:1], 0.0))
            dve.wait_ge(const_in, 16)
            dve.wait_ge(prm_in, 16)
            for t, (t0, n) in enumerate(tok):
                dve.wait_ge(xsq, t + 1)
                L(tv.reciprocal(st4[0:n, t:t + 1], st4[0:n, t:t + 1]))
                ts_(xn[0:n, t, :], xn[0:n, t, :], st4[0:n, t:t + 1], None, ALU.mult).then_inc(xnorm, 1)
            for t, (t0, n) in enumerate(tok):
                for h in range(2):
                    filled(dve, ("xT", t, h))
                    b = bank(("xT", t, h))[:, :].rearrange("p (c n) -> p c n", c=4)[:, :, 0:n]
                    i = tt_(xT[:, 4 * h:4 * h + 4, t0:t0 + n], b,
                            bc(prmv("norm_mix")[:, 4 * h:4 * h + 4].unsqueeze(2), P, 4, n), ALU.mult)
                    empties(i, ("xT", t, h))
            dve.wait_ge(shift_in, 16)
            for f in [12, 13] + list(range(12)):
                dst = ps[:, f, :] if f < 12 else lx[:, f - 12, :]
                evacuated(dve, ("pT", f))
                tt_(dst[:, 0:SEQ], pT[:, f, 0:SEQ], pT[:, f, 1:SEQ + 1], ALU.subtract)
                L(tt_(dst[:, SEQ:T], Un[:, f * NB:(f + 1) * NB], pT[:, f, SEQ + 1:T + 1], ALU.subtract))
                i = stt(dst, dst, prmv("mu")[:, f:f + 1], pT[:, f, 1:T + 1], ALU.mult, ALU.add)
                if f == 13:
                    i.then_inc(shifted, 1)
            L(i)
            tv.tensor_copy(shout, pT[:, :, SEQ:T + 1]).then_inc(shift_out_ready, 1)
            dve.wait_ge(shift_out_ready, 1)
            kraw, r, v = ps[:, 4:8, :], ps[:, 0:4, :], ps[:, 8:12, :]
            L(tt_(F_kk[:], kraw, bc(prmv("k_k").unsqueeze(2), P, 4, T), ALU.mult))
            tt_(F_E, F_kk[:], F_kk[:], ALU.mult).then_inc(kk_sq, 1)
            for p in range(4):
                evacuated(dve, ("dec", p))
            L(ts_(F_logw, F_logw, -EXPM05, None, ALU.mult))
            for p in range(4):
                filled(dve, ("ss", p))
                empties(ts_(F_C[:, p, :], bank(("ss", p))[:, 0:T], 1e-24, None, ALU.max), ("ss", p))
            dve.wait_ge(kk_norm, 1)
            L(tv.reciprocal(F_C[:], F_C[:]))
            L(tt_(F_kk[:], F_kk[:], F_C[:], ALU.mult))
            for p in range(4):
                evacuated(dve, ("aaa", p))
            for p in range(4):
                i = ts_(F_C[:, p, :], F_a[:, p, :], 1.0, prmv("k_a")[:, p:p + 1], ALU.subtract, ALU.mult)
            L(i)
            L(stt(kraw, F_C[:], 1.0, kraw, ALU.add, ALU.mult))
            L(tt_(F_a[:], F_kk[:], F_a[:], ALU.mult))
            for p in range(4):
                i = stt(F_E[:, p, :], r[:, p, :], prmv("r_k")[:, p:p + 1], kraw[:, p, :], ALU.mult, ALU.mult)
            i.then_inc(rk_done, 1)

            def rope(t):
                n = tok[t][1]
                for part in range(3):
                    evacuated(dve, ("qkv", part, t))
                src = stage[0:n, t, :].rearrange("p (h d) -> p h d", d=DH)
                tab = C("rope", 32)[:, 16 * t:16 * t + 16] if t < 2 else C("rope_s", 16, NB)
                cos, sin = [bc(tab[:, k:k + 8].unsqueeze(1), n, 16, 8) for k in (0, 8)]
                x1, x2 = src[:, :, 0:8], src[:, :, 8:16]
                q = [r16[0:n, k] for k in range(4)]
                tt_(q[0], x1, cos, ALU.mult)
                tt_(q[1], x2, sin, ALU.mult)
                tt_(q[2], x2, cos, ALU.mult)
                L(tt_(q[3], x1, sin, ALU.mult))
                tt_(x1, q[0], q[1], ALU.subtract)
                tt_(x2, q[2], q[3], ALU.add).then_inc(roped, 1)
                dve.wait_ge(roped, t + 1)

            def qkT_copy(t):
                t0, n = tok[t]
                for w in range(2):
                    job = ("qkT", t, w)
                    filled(dve, job)
                    empties(tv.tensor_copy(qkT[:, 4 * w:4 * w + 4, t0:t0 + n], bank4(job)[:, :, 0:n]), job)

            rope(0)
            for p in range(4):
                filled(dve, ("bon", p))
                i = tt_(F_bonus[:, p, :], bank(("bon", p))[:, 0:T], v[:, p, :], ALU.mult)
                empties(i, ("bon", p))
            evacuated(dve, ("bon", 3))
            for p in range(4):
                i = tv.tensor_tensor_scan(F_C[:, p, 0:SEQ], C("scan", SEQ), F_logw[:, p, 0:SEQ], 0.0, ALU.mult, ALU.add)
            L(i)
            tt_(F_E[:, :, 0:SEQ], F_C[:, :, 0:SEQ], F_logw[:, :, 0:SEQ], ALU.subtract).then_inc(cum_ready, 1)
            dve.wait_ge(exp1, 1)
            pr = slice(0, SEQ)
            L(stt(F_kk[:, :, pr], F_kk[:, :, pr], -1.0, F_E[:, :, pr], ALU.mult, ALU.mult))
            dve.sem_inc(cum_ready, 1)
            dve.wait_ge(exp2, 1)
            tt_(F_a[:, :, pr], F_a[:, :, pr], F_logw[:, :, pr], ALU.mult)
            tt_(kraw[:, :, pr], kraw[:, :, pr], F_logw[:, :, pr], ALU.mult)
            tt_(r[:, :, pr], r[:, :, pr], F_E[:, :, pr], ALU.mult).then_inc(tilde, 1)
            tv.memset(SBD[:], 0.0).then_inc(state_ready, 1)
            qkT_copy(0)

            def a_matrices(tt, kinds):
                for hg in range(2):
                    hs = slice(4 * hg, 4 * hg + 4)
                    for k in kinds:
                        job = ("A", tt, hg, k)
                        filled(dve, job)
                        if k == 1:
                            empties(tt_(X[:, hs, :], bank4(job), mask4("lvl0L"), ALU.mult), job)
                            evacuated(dve, job)
                            L(tt_(X[:, hs, :], X[:, hs, :], mask4("ident"), ALU.add))
                            dve.sem_inc(x_init, 1)
                            continue
                        dst, m = {0: (MT, "strictU"), 2: (AzkT, "strictU"), 3: (ArbT, "inclU"), 4: (ArkT, "inclU")}[k]
                        empties(tt_(dst[:, hs, :], bank4(job), mask4(m), ALU.mult), job)
                        if k == 0:
                            evacuated(dve, job)
                            L(tt_(XT[:, hs, :], MT[:, hs, :], mask4("lvl0U"), ALU.mult))
                            L(tt_(XT[:, hs, :], XT[:, hs, :], mask4("ident"), ALU.add))

            def level_masks(lvl):
                for hg in range(2):
                    hs = slice(4 * hg, 4 * hg + 4)
                    if lvl > 1:
                        filled(dve, ("P", 1, lvl - 1, hg))
                    tt_(MTl[:, hs, :], MT[:, hs, :], mask4(f"lvl{lvl}U"), ALU.mult).then_inc(lvl_mask, 1)

            def level(tt, lvl):
                for hg in range(2):
                    hs = slice(4 * hg, 4 * hg + 4)
                    for k, dst in (("XP", X), ("XPT", XT)):
                        filled(dve, (k, tt, lvl, hg))
                        if lvl > 1:
                            evacuated(dve, (k, tt, lvl - 1, hg))
                        empties(tt_(dst[:, hs, :], dst[:, hs, :], bank4((k, tt, lvl, hg)), ALU.add), (k, tt, lvl, hg))

            def chunks(tt):
                evacuated(dve, ("U0", tt))
                if tt == 1:
                    filled(dve, ("yi", 0, 1))
                for c in (2 * tt, 2 * tt + 1):
                    rows = slice((c % 2) * 64, (c % 2) * 64 + 64)
                    filled(dve, ("U", c))
                    empties(tt_(Un[rows, :], bank(("U", c))[rows, :], Gn[rows, :], ALU.add), ("U", c))
                    filled(dve, ("dS", c))
                    empties(tt_(tmpY4, bank4(("dS", c)), mask4("blk"), ALU.mult), ("dS", c))
                    evacuated(dve, ("dS", c))
                    L(tt_(SBD[:], SBD[:], tmpY4, ALU.add))
                    tt_(SBD[:], SBD[:], bc(WC[:, :, c:c + 1], P, 4, P), ALU.mult).then_inc(state_ready, 1)
                    dve.wait_ge(state_ready, c + 2)

            def y_inner(tt):
                for c in (2 * tt, 2 * tt + 1):
                    evacuated(dve, ("ys", c))
                for hf in range(2):
                    job = ("yi", tt, hf)
                    filled(dve, job)
                    bv = bank(job)[:, :].rearrange("p (a r t) -> p a r t", a=2, r=2)
                    for par in range(2):
                        rw = slice(par * 64, par * 64 + 64)
                        y = F_y[rw, 2 * hf:2 * hf + 2, tt * P:(tt + 1) * P]
                        i = tt_(y, y, bv[rw, :, par, :], ALU.add)
                    empties(i, job)
                evacuated(dve, ("yi", tt, 1))
                dve.sem_inc(y_done[tt], 1)

            def y_post(t):
                n = tok[t][1]
                y, tmp = F_y[:, :, cols(t)], grid(tmpY, 0, 4, n)
                filled(dve, ("mean", t))
                empties(stt(y, bank4(("mean", t), n), -1.0 / DH, y, ALU.mult, ALU.add), ("mean", t))
                evacuated(dve, ("mean", t))
                tt_(tmp, y, y, ALU.mult).then_inc(ysq_ready, 1)
                filled(dve, ("var", t))
                empties(ts_(tmp, bank4(("var", t), n), 1.0 / DH, GN_EPS, ALU.mult, ALU.add), ("var", t))
                evacuated(dve, ("var", t))
                dve.sem_inc(gn_var, 1)
                dve.wait_ge(gn_std, t + 1)
                L(tv.reciprocal(tmp, tmp))
                L(tt_(y, y, tmp, ALU.mult))
                L(tt_(y, y, bc(prmv("gn_g").unsqueeze(2), P, 4, n), ALU.mult))
                L(tt_(y, y, bc(prmv("gn_b").unsqueeze(2), P, 4, n), ALU.add))
                L(tt_(y, y, F_bonus[:, :, cols(t)], ALU.add))
                tt_(cat[:, 0:4, cols(t)], y, F_g[:, :, cols(t)], ALU.mult).then_inc(cat_ready, 1)

            def att_a(u):
                nh = 4 if u < 2 else 2
                job = ("S", u)
                filled(dve, job)
                if u < 2:
                    i = tt_(att_s, bank4(job), mask4("causal"), ALU.add)
                else:
                    bv = bank4(job).rearrange("p (h k) t -> p h k t", k=2)
                    av = att_s.rearrange("p (h k) t -> p h k t", k=2)
                    tv.tensor_copy(av[:, :, 0, :], bv[:, :, 0, :])
                    i = tt_(av[:, :, 1, :], bv[:, :, 1, :], bc(C("causal").unsqueeze(1), P, 2, P), ALU.add)
                empties(i, job)
                evacuated(dve, job)
                flat = att_s.rearrange("p a b -> p (a b)").rearrange("p (h w) -> p h w", h=nh)
                L(tv.reduce_max(st4[:, 4:4 + nh], flat, axis=AX))
                ts_(st4[:, 4:4 + nh], st4[:, 4:4 + nh], -SCALE, None, ALU.mult).then_inc(att_masked, 1)

            def att_b(u):
                nh = 4 if u < 2 else 2
                flat = att_s.rearrange("p a b -> p (a b)").rearrange("p (h w) -> p h w", h=nh)
                dve.wait_ge(att_exp, u + 1)
                L(tv.reciprocal(st4[:, 8:8 + nh], st4[:, 8:8 + nh]))
                if u:
                    filled(dve, ("PT", u - 1))
                else:
                    dve.wait_ge(out_shift, 16)
                tt_(att_p.rearrange("p a b -> p (a b)").rearrange("p (h w) -> p h w", h=nh), flat,
                    bc(st4[:, 8:8 + nh].unsqueeze(2), P, nh, 512 // nh), ALU.mult).then_inc(att_norm, 1)
                dve.wait_ge(att_norm, u + 1)

            def att_c(u):
                filled(dve, ("PV", u))
                for n in range(4 if u < 2 else 2):
                    h = unit(u)[n if u < 2 else 2 * n][0]
                    r0 = (h % 2) * 64
                    q0 = 0 if u < 2 else P
                    i = tv.tensor_copy(cat[r0:r0 + 64, 4 + h // 2, q0:q0 + P], bank(("PV", u))[r0:r0 + 64, n * P:(n + 1) * P])
                empties(i, ("PV", u))

            def residual(t, hf):
                n = tok[t][1]
                job = ("h", t, hf)
                filled(dve, job)
                dve.wait_ge(x2_in[t], 16)
                part = slice(hf * 512, (hf + 1) * 512)
                empties(tt_(hb[0:n, t, part], hb[0:n, t, part], bank(job)[0:n, :], ALU.add), job)
                if hf == 1:
                    evacuated(dve, job)
                    dve.sem_inc(h_ready, 1)

            def norm(t):
                n = tok[t][1]
                dve.wait_ge(gain_in, 16)
                dve.wait_ge(h_sq, t + 1)
                L(tv.reciprocal(st4[0:n, t:t + 1], st4[0:n, t:t + 1]))
                stt(xf[0:n, t, :], hb[0:n, t, :], st4[0:n, t:t + 1], gain[0:n, :], ALU.mult, ALU.mult).then_inc(xf_ready, 1)

            def xfT_copy(t):
                g = min(t, 1)
                o, n = tok[t][0] - grp[g][0], tok[t][1]
                for h in range(2):
                    job = ("xfT", t, h)
                    filled(dve, job)
                    empties(tv.tensor_copy(xfTg(g)[:, 4 * h:4 * h + 4, o:o + n], bank4(job)[:, :, 0:n]), job)

            def top16(n, src, val, ind, job=None):
                w = src[0].shape[-1]
                for k in range(4):
                    i = tv.max(val[k][:, 0:8], src[k])
                L(i)
                for k in range(4):
                    tv.max_index(ind[k][:, 0:8], val[k][:, 0:8], src[k])
                for k in range(4):
                    i = tv.match_replace(work[0:n, k, 0:w], val[k][:, 0:8], src[k], -3.0e38)
                if job:
                    empties(i, job)
                    evacuated(dve, job)
                else:
                    L(i)
                for k in range(4):
                    i = tv.max(val[k][:, 8:16], work[0:n, k, 0:w])
                L(i)
                for k in range(4):
                    i = tv.max_index(ind[k][:, 8:16], val[k][:, 8:16], work[0:n, k, 0:w])
                L(i)

            def rank_halves(t, q):
                n = tok[t][1]
                R, job = slice(0, n), ("sc", t, q)
                filled(dve, job)
                top16(n, [bank(job)[R, k * P:(k + 1) * P] for k in range(4)], [sv[R, 4 * q + k, :] for k in range(4)],
                      [si_u[R, 4 * q + k, :] for k in range(4)], job)

            def route(t):
                n = tok[t][1]
                R = slice(0, n)
                if t == 1:
                    filled(dve, ("sc", 2, 3))
                L(tv.tensor_copy(sif[R], si_u[R]))
                svv = sv[R].rearrange("p (h k) a -> p h k a", k=2)
                c4 = comb[R].rearrange("p h (a b) -> p h a b", a=16)
                L(tt_(c4, bc(svv[:, :, 0, :].unsqueeze(3), n, 8, 16, 16), bc(svv[:, :, 1, :].unsqueeze(2), n, 8, 16, 16), ALU.add))
                civ = ci_u[R, :].rearrange("p (h k) -> p h k", h=8)
                for h in (0, 4):
                    top16(n, [comb[R, h + k, :] for k in range(4)], [cs[R, h + k, :] for k in range(4)],
                          [civ[:, h + k, :] for k in range(4)])
                gv = (gate[R, t, :] if t < 2 else gateS[:, :]).rearrange("p (h k) -> p h k", h=8)
                tt_(gv, cs[R], bc(cs[R, :, 0:1], n, 8, 16), ALU.subtract).then_inc(cs_ready, 1)
                ts_(hi_u[R, :], ci_u[R, :], 4, None, ALU.logical_shift_right)
                L(ts_(ci_u[R, :], ci_u[R, :], 15, None, ALU.bitwise_and))
                tv.tensor_copy(ehi[R], hi_u[R, :])
                L(tv.tensor_copy(elo[R], ci_u[R, :]))
                siv = sif[R].rearrange("p (h k) a -> p h k a", k=2)
                oh4 = oh[R].rearrange("p (h k) a -> p h k a", h=8)
                for k, src, dst in ((0, ehi, e1), (1, elo, e2)):
                    L(tt_(oh[R], bc(src[R].unsqueeze(2), n, NJ, 16), bc(C("iota16", 16, n).unsqueeze(1), n, NJ, 16), ALU.is_equal))
                    L(tt_(oh4, oh4, bc(siv[:, :, k, :].unsqueeze(2), n, 8, 16, 16), ALU.mult))
                    L(tv.reduce_sum(dst[R], oh[R], axis=AX))
                L(stt(idxf[R], e1[R], float(NKEYS), e2[R], ALU.mult, ALU.add))
                if t < 2:
                    L(tv.tensor_copy(idx[:, t, :], idxf))
                    dve.sem_inc(routed, 1)
                dve.wait_ge(g_exp, t + 1)
                L(tv.reduce_sum(mx8[R, 0:8], gv, axis=AX))
                L(tv.reciprocal(mx8[R, 0:8], mx8[R, 0:8]))
                L(tt_(gv, gv, bc(mx8[R, 0:8].unsqueeze(2), n, 8, 16), ALU.mult))
                if t == 2:
                    dve.sem_inc(routed, 1)

            a_matrices(0, (0, 1, 2))
            att_a(0)
            level(0, 1)
            att_b(0)
            level(0, 2)
            att_c(0)
            att_a(1)
            level(0, 3)
            att_b(1)
            level(0, 4)
            att_c(1)
            level(0, 5)
            a_matrices(0, (3, 4))
            chunks(0)
            y_inner(0)
            y_post(0)
            residual(0, 0)
            residual(0, 1)
            rope(1)
            rope(2)
            norm(0)
            qkT_copy(1)
            qkT_copy(2)
            xfT_copy(0)
            L(tv.memset(Qz, 0.0))
            evacuated(dve, ("qkT", 2, 0))
            for c in range(4):
                for par in range(2):
                    r0 = par * 64
                    o = 2 * c + par
                    z = Qz[r0:r0 + 64, c, :, :].rearrange("p b x -> p (b x)")
                    i = tv.tensor_copy(z[:, o:o + 72 * 7 + 1:72], qkT[r0:r0 + 64, c, SEQ:T])
            i.then_inc(q_spread, 1)
            filled(dve, ("own",))
            empties(tv.tensor_copy(g64[:, 32:33], bank(("own",))[0:64, 0:1]), ("own",))
            for q in range(4):
                rank_halves(0, q)
            route(0)

            def smp(region, i):
                return bc(region[:, i, SEQ:T].unsqueeze(2), P, NB, DH)

            def bank_s(job):
                return bank(job)[:, :].rearrange("p (b v) -> p b v", b=NB)

            dup = bc(C("dup64", DH).unsqueeze(1), P, NB, DH)

            def state_a():
                dve.wait_ge(state_in, 16)
                for i in range(4):
                    tt_(St[:, i], Ss[:, i], smp(F_kk, i), ALU.mult).then_inc(sst_ready, 1)
                for i in range(4):
                    filled(dve, ("sE", 0, i))
                    empties(tt_(St[:, i], bank_s(("sE", 0, i)), smp(F_a, i), ALU.mult), ("sE", 0, i))
                    L(tt_(Ss[:, i], Ss[:, i], bc(sw[:, i, :].unsqueeze(2), P, NB, DH), ALU.mult))
                    evacuated(dve, ("sE", 0, i))
                    L(tt_(Ss[:, i], Ss[:, i], St[:, i], ALU.subtract))
                    tt_(St[:, i], dup, smp(Vs, i), ALU.mult).then_inc(sst_ready, 1)

            def state_b():
                for i in range(4):
                    filled(dve, ("sE", 1, i))
                    empties(tt_(St[:, i], bank_s(("sE", 1, i)), smp(Ks, i), ALU.mult), ("sE", 1, i))
                    evacuated(dve, ("sE", 1, i))
                    L(tt_(Ss[:, i], Ss[:, i], St[:, i], ALU.add))
                    tt_(St[:, i], Ss[:, i], smp(Rs, i), ALU.mult).then_inc(sst_ready, 1)
                dve.sem_inc(sst_done, 1)
                for i in range(4):
                    filled(dve, ("sE", 2, i))
                    empties(tt_(St[:, i], bank_s(("sE", 2, i)), dup, ALU.mult), ("sE", 2, i))
                    evacuated(dve, ("sE", 2, i))
                    L(tv.reduce_sum(F_y[:, i, SEQ:T], St[:, i], axis=AX))
                dve.sem_inc(y_done[2], 1)

            def sample_softmax():
                dve.wait_ge(cache_used, 64)
                L(tv.tensor_copy(sc_s[0:64, :], pS[0:64, :]))
                sv3 = sc_s[0:64, :].rearrange("p (n k) -> p n k", n=8)
                L(tv.reduce_sum(g64[:, 0:8], sv3, axis=AX))
                cmp = g64b[:, :].rearrange("p (a b) -> p a b", a=8)
                tie = tie64.rearrange("p (a b) -> p a b", a=8)
                gi, gj = bc(g64[:, 0:8].unsqueeze(2), 64, 8, 8), bc(g64[:, 0:8].unsqueeze(1), 64, 8, 8)
                tt_(cmp, gj, gi, ALU.is_gt)
                L(tt_(tie, gj, gi, ALU.is_equal))
                L(tt_(tie, tie, C("lower8", 64, 64).rearrange("p (a b) -> p a b", a=8), ALU.mult))
                L(tt_(cmp, cmp, tie, ALU.add))
                L(tv.reduce_sum(g64[:, 8:16], cmp, axis=AX))
                L(ts_(g64[:, 16:24], g64[:, 8:16], 2.5, -BIG, ALU.is_gt, ALU.mult))
                L(tt_(sv3, sv3, bc(g64[:, 16:24].unsqueeze(2), 64, 8, 256), ALU.add))
                L(tv.reduce_max(g64[:, 36:37], sc_s[0:64, :], axis=AX))
                L(tt_(g64[:, 36:37], g64[:, 36:37], g64[:, 32:33], ALU.max))
                ts_(g64[:, 33:34], g64[:, 36:37], -SCALE, None, ALU.mult).then_inc(s_max, 1)
                dve.wait_ge(s_exp, 1)
                L(tt_(g64[:, 37:38], g64[:, 34:35], g64[:, 35:36], ALU.add))
                L(tv.reciprocal(g64[:, 37:38], g64[:, 37:38]))
                L(tt_(g64[:, 38:39], g64[:, 35:36], g64[:, 37:38], ALU.mult))
                L(ts_(g64b[:, :], ident[0:64, 0:64], g64[:, 38:39], None, ALU.mult))
                ts_(sc_s[0:64, :], sc_s[0:64, :], g64[:, 37:38], None, ALU.mult).then_inc(s_prob, 1)

            def sample_output():
                filled(dve, ("OT",))
                ov = bank(("OT",))[:, 0:8 * NB].rearrange("p (c b r) -> p c b r", c=4, r=2)
                tv.tensor_copy(cat[0:64, 4:8, SEQ:T], ov[0:64, :, :, 0])
                empties(tv.tensor_copy(cat[64:P, 4:8, SEQ:T], ov[64:P, :, :, 1]), ("OT",))

            def attention(u):
                att_a(u); att_b(u); att_c(u)

            def rows(t, kind, r0, r1):
                first = 32 * t + 16 * kind
                n0 = ch.n
                with dve.Fori(r0, r1) as rd:
                    ch.base, ch.n = rd + (n0 - r0), 0
                    col = bass.ds(rd * RS, RS)
                    if kind == 1:
                        L(tv.tensor_copy(w8[:], wgt[:, col]))
                    for s in range(RS):
                        dve.wait_ge(gathered[s], rd * 16 + 16 * (first + 1))
                        if kind == 0:
                            tv.tensor_tensor_reduce(out=ring[:, s, :], in0=ring[:, s, :], in1=xf[:, t, :], scale=1.0,
                                                    scalar=0.0, op0=ALU.mult, op1=ALU.add,
                                                    accum_out=act8[:, s:s + 1]).then_inc(row_used[s], 1)
                        else:
                            acc = (hb, xf)[s % 2][:, t, :]
                            if s >= 2:
                                dve.wait_ge(row_used[s - 2], rd + (first + 1))
                            stt(acc, ring[:, s, :], w8[:, s:s + 1], acc, ALU.mult, ALU.add).then_inc(row_used[s], 1)
                    if kind == 0:
                        dve.wait_ge(row_used[RS - 1], rd + (first + 1))
                        L(tv.tensor_copy(actv[:, col], act8[:, 0:RS]))
                    else:
                        dve.wait_ge(row_used[RS - 2], rd + (first + 1))
                        dve.wait_ge(row_used[RS - 1], rd + (first + 1))
                ch.base, ch.n = 0, n0 + (r1 - r0)

            def start_values(t):
                dve.wait_ge(gelu_done, t + 1)
                L(tt_(wgt[:], actv[:], gate[:, t, :], ALU.mult))
                L(tv.memset(xf[:, t, :], 0.0))

            def end_values(t):
                L(tt_(hb[:, t, :], hb[:, t, :], xf[:, t, :], ALU.add))
                dve.sem_inc(acc_ready, 1)

            def finish(t):
                n = tok[t][1]
                dve.wait_ge(y_sq, t + 1)
                dve.wait_ge(gain_in, 32)
                L(tv.reciprocal(st4[0:n, 12:13], st4[0:n, 12:13]))
                stt(xf[0:n, t, :], hb[0:n, t, :], st4[0:n, 12:13], gain[0:n, :], ALU.mult, ALU.mult).then_inc(y_ready, 1)

            def between(h):
                if h in (0, 1):
                    attention(2 + 2 * h)
                    attention(3 + 2 * h)
                elif h == 2:
                    state_a()
                elif h == 3:
                    state_b()
                elif h == 4:
                    dve.wait_ge(out_sstate, 16)
                    a_matrices(1, (0, 1, 2))
                    level_masks(1)
                elif h == 5:
                    sample_softmax()
                elif h in (6, 7, 8):
                    for lvl in {6: (1, 2), 7: (3,), 8: (4, 5)}[h]:
                        level(1, lvl)
                        if lvl < 5:
                            level_masks(lvl + 1)
                elif h == 9:
                    a_matrices(1, (3, 4))
                    chunks(1)
                elif h == 10:
                    y_inner(1)
                    y_post(1)
                elif h == 11:
                    sample_output()
                    y_post(2)
                elif h == 12:
                    for hf in range(2):
                        for t in (1, 2):
                            residual(t, hf)
                    norm(1)
                    norm(2)
                elif h == 13:
                    xfT_copy(1)
                    xfT_copy(2)
                elif h == 14:
                    rank_halves(1, 0)
                    rank_halves(1, 1)
                elif h == 15:
                    rank_halves(1, 2)
                    rank_halves(1, 3)
                    route(1)

            for h in range(2 * PEER_H):
                kind = h // PEER_H
                r0 = 2 * (h % PEER_H)
                rows(0, kind, r0, r0 + 2)
                if h == PEER_H - 1:
                    dve.sem_inc(u_done, 1)
                between(h)
                if h == PEER_H - 1:
                    start_values(0)
            end_values(0)
            rows(1, 0, 0, 2)
            rank_halves(2, 0)
            rank_halves(2, 1)
            rows(1, 0, 2, 4)
            rank_halves(2, 2)
            rank_halves(2, 3)
            rows(1, 0, 4, 6)
            route(2)
            rows(1, 0, 6, 8)
            finish(0)
            filled(dve, ("jT",))
            tv.tensor_copy(idxTs[:], bank(("jT",))[:, 0:NB])
            empties(tv.tensor_copy(gTs[:], bank(("jT",))[:, NB:2 * NB]), ("jT",))
            evacuated(dve, ("jT",))
            dve.sem_inc(sT_ready, 1)
            rows(1, 0, 8, 2 * PEER_H)
            dve.sem_inc(u_done, 1)
            start_values(1)
            rows(1, 1, 0, 2 * PEER_H)
            end_values(1)
            finish(1)
            for b in range(NB):
                dve.wait_ge(gathered[b], 16 * 65)
                for hf in range(2):
                    job = ("xb", b, hf)
                    filled(dve, job)
                    part = ring[:, b, hf * 512:(hf + 1) * 512]
                    empties(tv.tensor_tensor_reduce(out=part, in0=part, in1=bank(job)[:, :], scale=1.0, scalar=0.0,
                                                    op0=ALU.mult, op1=ALU.add,
                                                    accum_out=act8[:, hf * NB + b:hf * NB + b + 1]), job)
                    evacuated(dve, job)
                dve.sem_inc(row_used[b], 1)
            L(tt_(actS[:], act8[:, 0:NB], act8[:, NB:2 * NB], ALU.add))
            dve.sem_inc(u_done, 1)
            dve.wait_ge(gelu_done, 3)
            L(tv.memset(wSz[:], 0.0))
            L(tt_(actS[:], actS[:], gTs[:], ALU.mult))
            tv.tensor_copy(wSz[:].rearrange("p a b -> p (a b)")[:, 0:64:9], actS[:]).then_inc(w_ready, 1)
            dve.wait_ge(sv_done, 1)
            L(tt_(hb[0:NB, 2, :], hb[0:NB, 2, :], pS[0:NB, 0:D_MODEL], ALU.add))
            dve.sem_inc(acc_ready, 1)
            finish(2)


_OUTS = [("y_prompt", (SEQ, D_MODEL)), ("y_sample", (NB, D_MODEL)), ("k_prompt", (SEQ, W)), ("v_prompt", (SEQ, W)),
         ("wkv_prompt", (NH, DH, DH)), ("shiftT", (P, NF * (NB + 1))), ("k_sample", (NB, W)), ("v_sample", (NB, W)),
         ("wkv_sample", (P, NP4 * NB * DH))]


def kernel(**x):
    import concourse.bacc as bacc
    from concourse.bass_utils import run_bass_kernel_spmd

    x = {k: np.asarray(v) for k, v in x.items()}

    def feat(v):
        return v.reshape(-1, P).T

    ins = {
        "x_prompt": x["x_prompt"], "x_sample": x["x_sample"].reshape(NB, D_MODEL),
        "const": constants(), "const8": constants8(),
        "prm": np.concatenate([feat(x[n].reshape(-1)) for n in
                               ("mu_shift", "w0", "a0", "k_k", "k_a", "r_k", "gn_gain", "gn_bias", "norm_mix")], 1),
        "pages": x["page_table"].astype(np.int32).reshape(1, NB * NPAGE),
        "w_in": x["w_in"][0], "w_out": x["w_out"][0], "w_pq": x["w_pq"][0],
        "lora": np.concatenate([np.concatenate([x["w_decay_up"][0], x["w_aaa_up"][0]], 0), x["w_gate_up"][0]], 1),
        "shiftT": x["state_shift"][0].reshape(NB, NF, P).transpose(2, 1, 0).reshape(P, NF * NB),
        "state_wkv": x["state_wkv"][0].reshape(NB, NP4, 2, DH, DH).transpose(2, 4, 1, 0, 3).reshape(P, NP4 * NB * DH),
        "cache_k": x["cache_k"][0].reshape(N_POOL, PAGE, 4, P).transpose(0, 3, 2, 1).reshape(N_POOL, P, 4 * PAGE),
        "cache_v": x["cache_v"][0].reshape(N_POOL, PAGE, W),
        "subkT": x["peer_sub_keys"][0].transpose(2, 0, 1),
        "expert_u": x["expert_u"][0], "expert_v": x["expert_v"][0],
        "norm_ffn": x["norm_ffn"][0], "norm_final": x["norm_final"],
    }
    nc = bacc.Bacc("TRN2", target_bir_lowering=False, num_devices=1)
    arrays = {f"in_{n}": np.ascontiguousarray(a) for n, a in ins.items()}
    A = {n: nc.dram_tensor(f"in_{n}", arrays[f"in_{n}"].shape, mybir.dt.from_np(a.dtype), kind="ExternalInput").ap()
         for n, a in ins.items()}
    O = {n: nc.dram_tensor(f"out_{n}", shape, F32, kind="ExternalOutput").ap() for n, shape in _OUTS}
    step_kernel(nc, A, O)
    r = run_bass_kernel_spmd(nc, [arrays], core_ids=[0]).results[0]
    o = {n: r[f"out_{n}"] for n, _ in _OUTS}
    shift = o["shiftT"].reshape(P, NF, NB + 1).transpose(2, 1, 0).reshape(NB + 1, W_RWKV_IN)
    wkv = o["wkv_sample"].reshape(2, DH, NP4, NB, DH).transpose(3, 2, 0, 4, 1).reshape(1, NB, NH, DH, DH)
    return (o["y_prompt"].reshape(1, SEQ, D_MODEL), o["y_sample"].reshape(NB, 1, D_MODEL),
            o["k_prompt"].reshape(1, 1, SEQ, NH, DH), o["v_prompt"].reshape(1, 1, SEQ, NH, DH),
            o["wkv_prompt"].reshape(1, 1, NH, DH, DH), shift[0:1].reshape(1, 1, W_RWKV_IN),
            o["k_sample"].reshape(1, NB, 1, NH, DH), o["v_sample"].reshape(1, NB, 1, NH, DH),
            wkv, shift[1:].reshape(1, NB, W_RWKV_IN))
```

```python
import concourse.bass as bass
from concourse import mybir
from contextlib import ExitStack
import numpy as np

F32 = mybir.dt.float32
I32 = mybir.dt.int32
U32 = mybir.dt.uint32
ALU = mybir.AluOpType
ACT = mybir.ActivationFunctionType
AX = mybir.AxisListType.X

P = 128
D_MODEL, SEQ, NB, PAST, PAGE = 1024, 256, 8, 2048, 128
DH, NH = 64, 8
W = NH * DH
W_RWKV_IN = 3 * W + 256
NPAGE = PAST // PAGE
N_POOL = NB * NPAGE * 5 // 4
T = SEQ + NB
KC = D_MODEL // P
NF = W_RWKV_IN // P
NP4 = W // P
CHUNK = 64
NCH = SEQ // CHUNK
SCALE = DH ** -0.5
GN_EPS, NORM_EPS = 64e-5, 1e-6
PEER_H, NKEYS, TOPK = 8, 128, 16
NJ = PEER_H * TOPK
BIG = 1.0e30
EXPM05 = float(np.exp(np.float64(-0.5)))

C_MATS = ["ident", "blk", "strictU", "inclU", "lvl0L", "lvl0U",
          "lvl1U", "lvl2U", "lvl3U", "lvl4U", "lvl5U", "causal"]
C_OFF = {n: i * P for i, n in enumerate(C_MATS)}
_o = len(C_MATS) * P
for _n, _w in (("rope", 2 * 16), ("rope_s", 16), ("iota16", 16), ("lower8", 64), ("scan", SEQ),
               ("own8", NB), ("eps", 1), ("dup64", DH)):
    C_OFF[_n] = _o
    _o += _w
C_COLS = _o
PRM_W = [("mu", NF), ("w0", NP4), ("a0", NP4), ("k_k", NP4), ("k_a", NP4), ("r_k", NP4),
         ("gn_g", NP4), ("gn_b", NP4), ("norm_mix", KC)]
PRM_OFF, _o = {}, 0
for _n, _w in PRM_W:
    PRM_OFF[_n] = _o
    _o += _w
PRM_COLS = _o


def constants():
    c = np.zeros((P, C_COLS), np.float32)
    i, j = np.arange(P)[:, None], np.arange(P)[None, :]
    same = i // CHUNK == j // CHUNK

    def put(name, m):
        c[:m.shape[0], C_OFF[name]:C_OFF[name] + m.shape[1]] = m

    put("ident", i == j)
    put("blk", i // DH == j // DH)
    put("strictU", same & (i < j))
    put("inclU", same & (i <= j))
    for lvl in range(6):
        up = (i >> (lvl + 1) == j >> (lvl + 1)) & ((i >> lvl) % 2 == 0) & ((j >> lvl) % 2 == 1)
        put(f"lvl{lvl}U", up)
        if lvl == 0:
            put("lvl0L", up.T)
    put("causal", np.where(i >= j, 0.0, -BIG))
    inv = (1.0 / (np.float32(500000.0) ** (np.arange(8, dtype=np.float32) * np.float32(2.0) / np.float32(16)))).astype(np.float32)
    ang = (np.arange(SEQ, dtype=np.float32)[:, None] * inv[None]).astype(np.float32)
    rope = np.concatenate([np.cos(ang), np.sin(ang)], 1).astype(np.float32).reshape(2, P, 16)
    put("rope", rope.transpose(1, 0, 2).reshape(P, 32))
    ang = (np.float32(PAST) * inv).astype(np.float32)
    put("rope_s", np.tile(np.concatenate([np.cos(ang), np.sin(ang)])[None], (P, 1)))
    put("iota16", np.tile(np.arange(16)[None], (P, 1)))
    put("lower8", np.tile((np.arange(8)[None, :] < np.arange(8)[:, None]).reshape(1, 64), (P, 1)))
    put("scan", np.tile((np.arange(SEQ) % CHUNK != 0)[None], (P, 1)))
    put("eps", np.full((P, 1), NORM_EPS))
    put("dup64", i % DH == np.arange(DH)[None])
    put("own8", np.arange(64)[:, None] // 8 == np.arange(8)[None])
    return c


def constants8():
    return (np.arange(8)[:, None] == np.arange(NB * P)[None] // P).astype(np.float32)



W_LOADS = [("w_in", 3 * W)] + [("w_in", 256 * n) for n in range(6)] + \
    [("w_in", W_RWKV_IN + 256 * n) for n in range(6)]
QKV_LOAD = 7
H_LOAD = [13, 25]
Q_LOAD = [17, 29]
for _ in range(2):
    W_LOADS += [("w_out", 256 * n) for n in range(4)] + [("w_pq", 256 * n) for n in range(8)]
W_SLOT = [n % 6 for n in range(25)] + [4 + n % 2 for n in range(12)]
LATE = 8
SHARE = (2, 5, 7)
SHARED0 = 5


def shared_round(t, rd):
    return rd - SHARED0 if t == 0 else rd + (16 - SHARED0)


def uses_before(t, kind, rd):
    if (t, kind) != (1, 1):
        return {(0, 0): 0, (0, 1): 16, (1, 0): 32}[t, kind]
    return 48 + (rd >= 8) + (rd >= 10)


def last_use(n):
    if n == 0:
        return ("pT", 13)
    if n < QKV_LOAD:
        return ("pT", 2 * (n - 1) + 1)
    if n < H_LOAD[0]:
        return ("qkv", (n - QKV_LOAD) // 2, 1)
    for g, t in ((0, 0), (1, 2)):
        if n < Q_LOAD[g]:
            return ("h", t, (n - H_LOAD[g]) // 2)
        if n < Q_LOAD[g] + 8:
            return ("qT", g, n - Q_LOAD[g])


def schedule():
    o, count = [], [0]

    def halves(n):
        for _ in range(n):
            o.append(("cache", count[0] // 2, count[0] % 2))
            count[0] += 1

    def mixed(jobs, n):
        for i, x in enumerate(jobs):
            o.append(x)
            halves((i + 1) * n // len(jobs) - i * n // len(jobs))

    def rwkv(tt, fill):
        r = [("nat", tt, a) for a in range(4)]
        r += [("A", tt, hg, k) for hg in range(2) for k in range(3)]
        r += [("G", tt)]
        for lvl in range(1, 6):
            r += [("P", tt, lvl, hg) for hg in range(2)]
            r += fill[lvl - 1]
            r += [(k, tt, lvl, hg) for hg in range(2) for k in ("XP", "XPT")]
        r += [("U0", tt), ("TZ", tt, 0), ("TZ", tt, 1)]
        r += [("A", tt, hg, k) for hg in range(2) for k in (3, 4)]
        for c in (2 * tt, 2 * tt + 1):
            r += [("U", c), ("ys", c), ("dS", c)]
        return r + [("yi", tt, 0), ("yi", tt, 1)]

    o += [("xT", t, h) for t in range(3) for h in range(2)]
    o += [("pT", f) for f in [12, 13] + list(range(12))]
    o += [("dec", p) for p in range(4)] + [("aaa", p) for p in range(4)] + [("gate", p) for p in range(4)]
    o += [("qkv", 0, 0)] + [("ss", p) for p in range(4)] + [("qkv", 1, 0), ("qkv", 2, 0)]
    o += [("bon", p) for p in range(4)]
    o += [("qkv", part, 2) for part in range(3)]
    o += [("qkT", 0, 0), ("qkT", 0, 1), ("qkT", 2, 0), ("qkT", 2, 1)]
    front = rwkv(0, [[("S", 0), ("qkv", 0, 1)], [("PT", 0), ("qkv", 1, 1)], [("PV", 0), ("S", 1), ("qkv", 2, 1)],
                     [("PT", 1)], [("PV", 1)]])
    front += [("mean", 0), ("var", 0), ("h", 0, 0), ("h", 0, 1), ("qkT", 1, 0), ("qkT", 1, 1), ("own",)]
    front += [("xfT", 0, 0), ("xfT", 0, 1)]
    mixed(front, 16)
    o += [("qT", 0, j) for j in range(8)]
    mixed([("sc", 0, q) for q in range(4)], 12)
    o += [("S", 2)]
    halves(22)
    mixed([("sE", 0, i) for i in range(4)] + [("PT", 2), ("PV", 2), ("S", 3)], 64 - count[0])
    o += [("sE", 1, i) for i in range(4)] + [("PT", 3), ("PTs", 0), ("PTs", 1), ("poD",)]
    mixed([("PV", 3), ("S", 4)] + [("sE", 2, i) for i in range(4)] +
          [("PT", 4), ("PV", 4), ("S", 5), ("PT", 5), ("PV", 5)], 22)
    mixed(rwkv(1, [[], [], [], [], []]), 38)
    mixed([("Sout",), ("mean", 1), ("var", 1)], 128 - count[0])
    o += [("OT",), ("mean", 2), ("var", 2)]
    o += [("v", 0, 5), ("h", 1, 0), ("h", 2, 0), ("v", 0, 6), ("h", 1, 1), ("h", 2, 1), ("v", 0, 7)]
    o += [("xfT", t, h) for t in (1, 2) for h in range(2)] + [("v", 0, 8), ("qT", 1, 0), ("qT", 1, 1)]
    o += [("v", 0, 9), ("sc", 1, 0), ("qT", 1, 2), ("qT", 1, 3)]
    o += [("v", 0, 10), ("sc", 1, 1), ("qT", 1, 4), ("qT", 1, 5)]
    o += [("v", 0, 11), ("sc", 1, 2), ("qT", 1, 6), ("qT", 1, 7)]
    o += [("v", 0, 12), ("sc", 1, 3)] + [("sc", 2, q) for q in range(4)] + [("v", 0, n) for n in (13, 14, 15)]
    o += [("v", 1, n) for n in range(7)] + [("jT",), ("v", 1, 7)]
    for b in range(NB):
        o += [("xb", b, 0), ("xb", b, 1)]
    o += [("v", 1, 8), ("v", 1, 9)]
    return o


def bc(ap, *shape):
    return ap.broadcast_to(list(shape))


class Chain:

    def __init__(self, eng, sem):
        self.eng, self.sem, self.base, self.n = eng, sem, 0, 0

    def inc(self, ins):
        ins.then_inc(self.sem, 1)
        self.n += 1

    def wait(self):
        self.eng.wait_ge(self.sem, self.base + self.n)

    def link(self, ins):
        self.inc(ins)
        self.wait()


def step_kernel(nc, A, O):
    ctx = ExitStack()
    with ctx:
        def sb(name, shape, dt=F32):
            return ctx.enter_context(nc.sbuf_tensor(name, shape, dt))

        def sem(name):
            return ctx.enter_context(nc.semaphore(name))

        const = sb("const", [P, C_COLS])

        def C(name, w=P, rows=P):
            return const[0:rows, C_OFF[name]:C_OFF[name] + w]

        ident = C("ident")
        prm = sb("prm", [P, PRM_COLS])

        def prmv(name):
            return prm[:, PRM_OFF[name]:PRM_OFF[name] + dict(PRM_W)[name]]

        def grid(region, off, *dims):
            v = region[:, off:off + int(np.prod(dims))]
            names = [chr(97 + i) for i in range(len(dims))]
            if len(dims) == 1:
                return v
            return v.rearrange(f"p ({' '.join(names)}) -> p {' '.join(names)}", **dict(zip(names[1:], dims[1:])))

        RS = 8
        ring = sb("ring", [P, 12, 1024])
        wslot = [ring[:, 2 * s:2 * s + 2, :].rearrange("p a b -> p (a b)").rearrange("p (c n) -> p c n", c=KC)
                 for s in range(6)]
        cache = sb("cache", [P, 4, 512])
        xT = sb("xT", [P, KC, T])
        qkT = xT
        GN = P + NB
        tmpY = sb("tmpY", [P, 512])
        tmpY4 = grid(tmpY, 0, 4, P)
        amr = sb("amr", [P, 6144])
        MT, X, XT, MTl, AzkT, PM = [grid(amr, 1024 * k, NH, P) for k in range(6)]
        ArbT, ArkT = MT, MTl
        r16 = grid(amr, 0, 4, 16, 8)
        Ss, St = grid(amr, 0, 4, NB, DH), grid(amr, 2048, 4, NB, DH)
        qT = amr[:, 0:16 * GN]
        comb = grid(amr, 0, 8, 256)
        oh = grid(amr, 0, NJ, 16)
        RO = 16 * GN
        sv = grid(amr, RO, 16, 16)
        si_u = grid(amr, RO + 256, 16, 16).bitcast(U32)
        sif = grid(amr, RO + 512, 16, 16)
        cs = grid(amr, RO + 768, 8, 16)
        ehi, elo, e1, e2, idxf = [amr[:, RO + 896 + 128 * k:RO + 1024 + 128 * k] for k in range(5)]
        ci_u, hi_u = [amr[:, RO + 1536 + 128 * k:RO + 1664 + 128 * k].bitcast(U32) for k in range(2)]
        mx8 = amr[:, RO + 1792:RO + 1800]
        work = grid(amr, RO + 1800, 4, 256)
        ps = sb("ps", [P, 12, T])
        F_a, F_g, F_kk, F_C, F_bonus = [sb(n, [P, NP4, T]) for n in ("F_a", "F_g", "F_kk", "F_C", "F_bonus")]
        F_y = F_C
        hx = sb("hx", [P, 6144])
        pT = grid(hx, 0, NF, T + 1)
        lx = grid(hx, NF * (T + 1), 2, T)
        F_logw = grid(hx, NF * (T + 1) + 2 * T, NP4, T)
        F_E = grid(hx, 0, NP4, T)
        hb = grid(hx, 0, 3, D_MODEL)
        xf = grid(hx, 3072, 3, D_MODEL)
        Qz = grid(hx, 4096, 4, NB, 64)
        PTs = grid(hx, 4096, NPAGE, 64)
        sc_s = hx[:, 1024:3072]
        stage = sb("stage", [P, 3, 2 * W])
        xn = stage[:, :, :]
        vN = sb("vN", [P, 3, W])
        Un, Gn = sb("Un", [P, W]), sb("Gn", [P, W])
        TZT, SBD = sb("TZT", [P, NP4, P]), sb("SBD", [P, NP4, P])
        att_s, att_p, att_t = grid(Un, 0, 4, P), TZT[:], tmpY4
        shout = TZT[:, :, :].rearrange("p a b -> p (a b)")[:, 0:NF * (NB + 1)].rearrange("p (a b) -> p a b", a=NF)
        cat = sb("cat", [P, 2 * NP4, T])
        loraW = cat[:, :, :].rearrange("p a b -> p (a b)")[:, 0:2 * W]
        nat = sb("nat", [P, 4, W])
        xfT = nat[:, :, :].rearrange("p a b -> p (a b)")
        diag = TZT
        gain = sb("gain", [P, D_MODEL])
        sel8 = ps[0:NB, 0:4, :].rearrange("p a b -> p (a b)")[:, 0:NB * P]
        subk = sb("subk", [P, 2, P])
        pg = sb("pg", [1, NB * NPAGE], I32)
        sw, WC = sb("sw", [P, NP4, NB]), sb("WC", [P, NP4, NCH])
        g64, g64b = sb("g64", [64, 40]), sb("g64b", [64, 64])
        tie64 = Gn[0:64, 0:64]
        small = sb("small", [NB, 64])
        st4 = sb("st4", [P, 16])
        idx = sb("idx", [P, 2, NJ], I32)
        idxh = sb("idxh", [P, 2, RS], I32)
        idxTs = sb("idxTs", [P, NB], I32)
        gate = sb("gate", [P, 2, NJ])
        gateS = F_g[0:NB, 0, 0:NJ]
        actv, wgt = sb("actv", [P, NJ]), sb("wgt", [P, NJ])
        act8, w8 = sb("act8", [P, 2 * RS]), sb("w8", [P, RS])
        gTs, actS = sb("gTs", [P, NB]), sb("actS", [P, NB])
        wSz = sb("wSz", [P, NB, NB])

        pS = ctx.enter_context(nc.psum_tensor("pS", [P, 2048], F32))
        pR = [ctx.enter_context(nc.psum_tensor(f"pR{i}", [P, 512], F32)) for i in range(4)]

        (const_in, prm_in, page_in, lora_in, gain_in, subk_in, sel8_in, shift_in, state_in) = [sem(n) for n in (
            "const_in", "prm_in", "page_in", "lora_in", "gain_in", "subk_in", "sel8_in", "shift_in", "state_in")]
        x_in = [sem(f"x_in{t}") for t in range(3)]
        x2_in = [sem(f"x2_in{t}") for t in range(3)]
        w_in_sem = [sem(f"w_in{s}") for s in range(6)]
        bank_filled = [sem(f"bank_filled{i}") for i in range(4)]
        bank_emptied = [sem(f"bank_emptied{i}") for i in range(4)]
        dve_step, act_step = sem("dve_step"), sem("act_step")
        (xsq, xnorm, q_spread, att_masked, att_exp, att_norm) = [sem(n) for n in (
            "xsq", "xnorm", "q_spread", "att_masked", "att_exp", "att_norm")]
        (shifted, lora_act, kk_sq, kk_norm, rk_done, cum_ready, exp1, exp2, tilde) = [sem(n) for n in (
            "shifted", "lora_act", "kk_sq", "kk_norm", "rk_done", "cum_ready", "exp1", "exp2", "tilde")]
        (lvl_mask, x_init, state_ready, ysq_ready, gn_var, gn_std) = [sem(n) for n in (
            "lvl_mask", "x_init", "state_ready", "ysq_ready", "gn_var", "gn_std")]
        y_done = [sem(f"y_done{t}") for t in range(3)]
        roped = [sem(f"roped{t}") for t in range(3)]
        cat_ready = sem("cat_ready")
        cache_in = [sem(f"cache_in{i}") for i in range(4)]
        late_in = [sem(f"late_in{i}") for i in range(6)]
        cache_used = sem("cache_used")
        s_max, s_exp, s_prob, o_done, o_copied = [sem(n) for n in ("s_max", "s_exp", "s_prob", "o_done", "o_copied")]
        sst_ready, sst_done = sem("sst_ready"), sem("sst_done")
        h_ready, h_sq, xf_ready = sem("h_ready"), sem("h_sq"), sem("xf_ready")
        routed, cs_ready, g_exp = sem("routed"), sem("cs_ready"), sem("g_exp")
        idx_moved, slot_open = sem("idx_moved"), sem("slot_open")
        gathered = [sem(f"gathered{i}") for i in range(RS)]
        row_used = [sem(f"row_used{i}") for i in range(RS)]
        w8_ready, diag_ready = sem("w8_ready"), sem("diag_ready")
        u_done, gelu_done, w_ready = sem("u_done"), sem("gelu_done"), sem("w_ready")
        sT_ready = sem("sT_ready")
        acc_ready, y_sq, y_ready = sem("acc_ready"), sem("y_sq"), sem("y_ready")
        out_kv = [sem(f"out_kv{t}") for t in range(3)]
        out_shift, out_state, out_sstate, out_y = [sem(n) for n in ("out_shift", "out_state", "out_sstate", "out_y")]
        shift_out_ready, sout_copied = sem("shift_out_ready"), sem("sout_copied")

        order = schedule()
        jobs = [x for x in order if x[0] not in ("cache", "v")]
        J = {name: n for n, name in enumerate(jobs)}
        assert len(J) == len(jobs)

        def bank(job):
            return pR[J[job] % 4]

        def bank4(job, n=P):
            return bank(job)[:, 0:4 * n].rearrange("p (a b) -> p a b", a=4)

        def filled(eng, job):
            eng.wait_ge(bank_filled[J[job] % 4], J[job] // 4 + 1)

        def evacuated(eng, job):
            eng.wait_ge(bank_emptied[J[job] % 4], J[job] // 4 + 1)

        def empties(ins, job):
            ins.then_inc(bank_emptied[J[job] % 4], 1)

        tok = [(0, P), (P, P), (SEQ, NB)]
        grp = [(0, P, (0,)), (P, GN, (1, 2))]

        def cols(t):
            return slice(tok[t][0], tok[t][0] + tok[t][1])

        def w_arrived(eng, n):
            eng.wait_ge(w_in_sem[W_SLOT[n]], 16 * W_SLOT[:n + 1].count(W_SLOT[n]))

        def unit(u):
            if u < 2:
                return [(2 * n + u, 0) for n in range(4)]
            return [(4 * ((u - 2) // 2) + 2 * (n // 2) + u % 2, n % 2) for n in range(4)]

        def late_page(m, j, n=1):
            place = cache[:, :, :] if m == 0 else ring[:, 6 + 2 * m:8 + 2 * m, :]
            return place.rearrange("p a b -> p (a b)")[:, j * 512:(j + n) * 512]

        def xfTg(g):
            n = grp[g][1]
            return xfT[:, 0:KC * n].rearrange("p (c n) -> p c n", c=KC)

        def slot(h):
            return 4 * (h % 2) + h // 2

        def OmS(b):
            return stage[0:NH, b // 2, (b % 2) * W:(b % 2 + 1) * W] if b < 6 else sc_s[0:NH, (b - 6) * W:(b - 5) * W]

        Zs, Bs, Rs, Ks, Vs = F_kk, F_a, ps[:, 0:4, :], ps[:, 4:8, :], ps[:, 8:12, :]
        block = ctx.enter_context(nc.Block())
        tv, ta, tg = nc.vector, nc.scalar, nc.gpsimd

        @block.sync
        def _(sp):
            def load_w(n):
                name, c0 = W_LOADS[n]
                before = [m for m in range(n) if W_SLOT[m] == W_SLOT[n]]
                if n in (H_LOAD[1], H_LOAD[1] + 1):
                    sp.wait_ge(cache_used, 128)
                elif before:
                    filled(sp, last_use(before[-1]))
                sp.dma_start(wslot[W_SLOT[n]], A[name].rearrange("(c p) n -> p c n", p=P)[:, :, c0:c0 + 256])\
                    .then_inc(w_in_sem[W_SLOT[n]], 16)

            def load_keys(n0, n1):
                def one(n, first):
                    for j in range(4):
                        if j % 2 == 0 and not first:
                            sp.wait_ge(cache_used, n * 2 + (j // 2 - 1))
                        k = sp.value_load(pg[0:1, bass.ds(n * 4 + j, 1)], min_val=0, max_val=N_POOL - 1)
                        sp.dma_start(cache[:, j, :], A["cache_k"][bass.ds(k, 1)].rearrange("a p n -> p (a n)"))\
                            .then_inc(cache_in[j], 16)
                if n1 - n0 == 1:
                    one(n0, n0 == 0)
                else:
                    with sp.Fori(n0, n1) as n:
                        one(n, False)

            def load_late(src, g, m, first=False):
                page0 = (LATE + m) * 4 - (0 if src is A["cache_k"] else NB * NPAGE)
                for j in range(4):
                    if first and m > 0:
                        filled(sp, ("qT", 0, 7))
                    elif j % 2 == 0:
                        sp.wait_ge(cache_used, g * 6 + (2 * (LATE + m - (1 if first else 3)) + j // 2 + 1))
                    k = sp.value_load(pg[0:1, bass.ds(g * 12 + (page0 + j), 1)], min_val=0, max_val=N_POOL - 1)
                    sp.dma_start(late_page(m, j), src[bass.ds(k, 1)].rearrange("a p n -> p (a n)"))\
                        .then_inc(late_in[2 * m + j // 2], 16)

            sp.dma_start(xn[:, 0, :], A["x_prompt"][0, 0:P, :]).then_inc(x_in[0], 16)
            sp.dma_start(const[:], A["const"]).then_inc(const_in, 16)
            sp.dma_start(prm[:], A["prm"]).then_inc(prm_in, 16)
            load_w(0)
            sp.dma_start(xn[:, 1, :], A["x_prompt"][0, P:2 * P, :]).then_inc(x_in[1], 16)
            sp.dma_start(xn[0:NB, 2, :], A["x_sample"]).then_inc(x_in[2], 16)
            load_w(1)
            sp.dma_start(Un[:, 0:NF * NB], A["shiftT"]).then_inc(shift_in, 16)
            load_w(2)
            sp.dma_start(loraW, A["lora"]).then_inc(lora_in, 16)
            for n in range(3, 6):
                load_w(n)
            sp.dma_start(pg[:], A["pages"]).then_inc(page_in, 16)
            sp.dma_start(subk[:], A["subkT"]).then_inc(subk_in, 16)
            sp.dma_start(gain[:], A["norm_ffn"].partition_broadcast(P)).then_inc(gain_in, 16)
            for n in range(6, QKV_LOAD + 6):
                load_w(n)
            sp.wait_ge(page_in, 16)
            load_keys(0, 1)

            def store_kv(t):
                n = tok[t][1]
                ko, vo = (O["k_prompt"][t * P:(t + 1) * P, :], O["v_prompt"][t * P:(t + 1) * P, :]) if t < 2 else \
                    (O["k_sample"], O["v_sample"])
                sp.wait_ge(roped[t], 1)
                sp.dma_start(ko, stage[0:n, t, W:2 * W]).then_inc(out_kv[t], 16)
                sp.dma_start(vo, vN[0:n, t, :]).then_inc(out_kv[t], 16)

            sp.wait_ge(shift_out_ready, 1)
            sp.dma_start(O["shiftT"], shout.rearrange("p a b -> p (a b)")).then_inc(out_shift, 16)
            store_kv(0)
            store_kv(2)
            load_keys(1, 3)
            load_w(H_LOAD[0])
            load_w(H_LOAD[0] + 1)
            load_w(H_LOAD[0] + 2)
            load_w(H_LOAD[0] + 3)
            load_keys(3, 4)
            load_w(Q_LOAD[0])
            load_w(Q_LOAD[0] + 1)
            load_keys(4, 8)
            evacuated(sp, ("var", 0))
            sp.wait_ge(tilde, 1)
            sp.dma_start(hb[:, 0, :], A["x_prompt"][0, 0:P, :]).then_inc(x2_in[0], 16)
            load_w(Q_LOAD[0] + 2)
            load_w(Q_LOAD[0] + 3)
            load_w(Q_LOAD[0] + 4)
            load_w(Q_LOAD[0] + 5)
            store_kv(1)
            load_w(Q_LOAD[0] + 6)
            load_w(Q_LOAD[0] + 7)
            for m in range(3):
                load_late(A["cache_k"], 0, m, True)
            with sp.Fori(1, 5) as g:
                for m in range(3):
                    load_late(A["cache_k"], g, m)
            sp.wait_ge(routed, 1)
            sp.dma_start(Ss.rearrange("p a b v -> p (a b v)"), A["state_wkv"]).then_inc(state_in, 16)
            with sp.Fori(5, (32 - LATE) // 3) as g:
                for m in range(3):
                    load_late(A["cache_k"], g, m)
            for m in range(3):
                load_late(A["cache_v"], (32 - LATE) // 3, m)
            sp.wait_ge(sst_done, 1)
            sp.dma_start(O["wkv_sample"], Ss.rearrange("p a b v -> p (a b v)")).then_inc(out_sstate, 16)
            with sp.Fori((32 - LATE) // 3 + 1, (64 - LATE) // 3) as g:
                for m in range(3):
                    load_late(A["cache_v"], g, m)
            for m in range(2):
                load_late(A["cache_v"], (64 - LATE) // 3, m)
            load_w(H_LOAD[1])
            load_w(H_LOAD[1] + 1)
            sp.wait_ge(sout_copied, 1)
            so = Gn[:, :].rearrange("p (a b) -> p a b", a=NP4)
            for par in range(2):
                sp.dma_start(O["wkv_prompt"].rearrange("(a r) v k -> r v a k", r=2)[par],
                             so[par * 64:par * 64 + 64, :, par * 64:par * 64 + 64]).then_inc(out_state, 16)
            sp.dma_start(sel8, A["const8"]).then_inc(sel8_in, 16)
            filled(sp, ("OT",))
            sp.dma_start(hb[:, 1, :], A["x_prompt"][0, P:2 * P, :]).then_inc(x2_in[1], 16)
            sp.dma_start(hb[0:NB, 2, :], A["x_sample"]).then_inc(x2_in[2], 16)
            for n in range(H_LOAD[1] + 2, Q_LOAD[1] + 8):
                load_w(n)
            sp.wait_ge(xf_ready, 3)
            sp.dma_start(gain[:], A["norm_final"].partition_broadcast(P)).then_inc(gain_in, 16)
            for n, t in enumerate((0, 2, 1)):
                sp.wait_ge(y_ready, n + 1)
                sp.dma_start(O["y_prompt"][t * P:(t + 1) * P, :] if t < 2 else O["y_sample"], xf[0:tok[t][1], t, :])\
                    .then_inc(out_y, 16)
            for t in range(3):
                sp.wait_ge(out_kv[t], 32)
            sp.wait_ge(out_shift, 16)
            sp.wait_ge(out_state, 32)
            sp.wait_ge(out_sstate, 16)
            sp.wait_ge(out_y, 48)

        @block.tensor
        def _(pe):
            mm, tr = nc.tensor.matmul, nc.tensor.transpose

            def begin(job):
                n = J[job]
                if n >= 4:
                    pe.wait_ge(bank_emptied[n % 4], n // 4)
                return pR[n % 4]

            def end(job, ins):
                ins.then_inc(bank_filled[J[job] % 4], 1)

            def j_xT(job, t, h):
                n = tok[t][1]
                pe.wait_ge(xnorm, t + 1)
                b = begin(job)
                for c in range(4):
                    i = tr(b[:, c * P:c * P + n], xn[0:n, t, (4 * h + c) * P:(4 * h + c + 1) * P], ident[0:n, 0:n])
                end(job, i)

            def j_pT(job, f):
                if f == 12:
                    for t in (1, 2):
                        for h in range(2):
                            evacuated(pe, ("xT", t, h))
                load, c0 = (0, (f - 12) * P) if f >= 12 else (1 + f // 2, (f % 2) * P)
                w_arrived(pe, load)
                b = begin(job)
                for c in range(KC):
                    i = mm(b[:, 0:T], wslot[W_SLOT[load]][:, c, c0:c0 + P], xT[:, c, :], start=(c == 0), stop=(c == KC - 1))
                end(job, i)

            def project(b, n, lhs, load0):
                for hf in range(2):
                    w_arrived(pe, load0 + hf)
                    for c in range(KC):
                        i = mm(b[0:n, hf * 256:(hf + 1) * 256], lhs(c), wslot[W_SLOT[load0 + hf]][:, c, :],
                               start=(c == 0), stop=(c == KC - 1))
                return i

            def j_qkv(job, part, t):
                t0, n = tok[t]
                b = begin(job)
                end(job, project(b, n, lambda c: xT[:, c, t0:t0 + n], QKV_LOAD + 2 * part))

            def j_qkT(job, t, w):
                n = tok[t][1]
                pe.wait_ge(roped[t], 1)
                b = begin(job)
                for p in range(4):
                    i = tr(b[:, p * P:p * P + n], stage[0:n, t, w * W + p * P:w * W + (p + 1) * P], ident[0:n, 0:n])
                end(job, i)

            def j_own(job):
                pe.wait_ge(q_spread, 1)
                evacuated(pe, ("qkT", 2, 1))
                b = begin(job)
                for s in range(NB):
                    for c in range(4):
                        i = mm(b[0:64, 0:1], Qz[:, c, s, :], qkT[:, 4 + c, SEQ + s:SEQ + s + 1],
                               start=(s == 0 and c == 0), stop=(s == NB - 1 and c == 3))
                end(job, i)

            def j_S(job, u):
                qt = 0 if u < 2 else 1
                evacuated(pe, ("qkT", qt, 0)); evacuated(pe, ("qkT", qt, 1))
                b = begin(job)
                for n, (h, kc) in enumerate(unit(u)):
                    r0 = (h % 2) * 64
                    i = mm(b[:, n * P:(n + 1) * P], qkT[r0:r0 + 64, h // 2, qt * P:(qt + 1) * P],
                           qkT[r0:r0 + 64, 4 + h // 2, kc * P:(kc + 1) * P], start=True, stop=True)
                end(job, i)

            def j_PT(job, u):
                pe.wait_ge(att_norm, u + 1)
                b = begin(job)
                for n in range(4):
                    i = tr(b[:, n * P:(n + 1) * P], att_p[:, n, :], ident)
                end(job, i)

            def j_PV(job, u):
                evacuated(pe, ("PT", u))
                evacuated(pe, ("qkv", 2, 0 if u < 2 else 1))
                b = begin(job)
                for n, (h, kc) in enumerate(unit(u)):
                    hh = n if u < 2 else n // 2
                    i = mm(b[:, hh * P:(hh + 1) * P], vN[:, kc, (h // 2) * P:(h // 2 + 1) * P],
                           att_t[:, n, :], start=(kc == 0), stop=(u < 2 or kc == 1))
                end(job, i)

            def half_unit(n, hf):
                b, g = (n % 32) // 4, n % 4
                if n == 0:
                    pe.wait_ge(q_spread, 1)
                if n == 32:
                    pe.wait_ge(s_prob, 1)
                    evacuated(pe, ("PTs", 0)); evacuated(pe, ("PTs", 1)); evacuated(pe, ("poD",))
                if n >= 32 and g == 0 and b >= 4 and hf == 0:
                    pe.wait_ge(o_copied, b - 3)
                place = 0 if n < LATE else (n - LATE) % 3
                if n < LATE:
                    pe.wait_ge(cache_in[2 * hf], 16 * (n + 1))
                    pe.wait_ge(cache_in[2 * hf + 1], 16 * (n + 1))
                else:
                    pe.wait_ge(late_in[2 * place + hf], 32 * ((n - LATE) // 3 + 1))
                if n < 32:
                    rhs = late_page(place, 2 * hf, 2).rearrange("p (a c t) -> p a c t", a=2, c=4)
                    for c in range(4):
                        i = mm(pS[0:64, g * 512 + hf * 256:g * 512 + (hf + 1) * 256], Qz[:, c, b, :], rhs[:, :, c, :],
                               start=(n < 4 and hf == 0 and c == 0), stop=(b == NB - 1 and c == 3),
                               skip_group_check=True)
                else:
                    o = pS[0:NH, (b % 4) * 512:(b % 4 + 1) * 512]
                    for j in (2 * hf, 2 * hf + 1):
                        i = mm(o, PTs[:, 4 * g + j, 8 * b:8 * b + 8], late_page(place, j),
                               start=(g == 0 and j == 0), stop=False, skip_group_check=True)
                i.then_inc(cache_used, 1)
                if n >= 32 and g == 3 and hf == 1:
                    mm(o, small[:, 8 * b:8 * b + 8], vN[0:NB, 2, :], start=False, stop=True,
                       skip_group_check=True).then_inc(o_done, 1)

            def value_rows(t, use, k, start=False, stop=False):
                if start and t == 1:
                    pe.wait_ge(acc_ready, 1)
                for n, s in enumerate(SHARE):
                    pe.wait_ge(gathered[s], use)
                    pe.wait_ge(diag_ready, k + n)
                    for hf in range(2):
                        i = mm(pS[:, hf * 512:(hf + 1) * 512], diag[:, n, :], ring[:, s, hf * 512:(hf + 1) * 512],
                               start=start and n == 0, stop=stop and s == SHARE[-1], skip_group_check=True)
                    i.then_inc(row_used[s], 1)

            def samples_rows():
                pe.wait_ge(w_ready, 1)
                for b in range(NB):
                    pe.wait_ge(gathered[b], 16 * 60)
                    for hf in range(2):
                        i = mm(pS[0:NB, 1024 + hf * 512:1024 + (hf + 1) * 512], wSz[:, b, :],
                               ring[:, b, hf * 512:(hf + 1) * 512], start=(b == 0), stop=(b == NB - 1),
                               skip_group_check=True)
                    i.then_inc(row_used[b], 1)

            def j_lora(job, p):
                rows, c0, rhs = {"dec": (slice(0, 64), 0, lx[0:64, 0, :]), "aaa": (slice(64, P), 0, lx[64:P, 0, :]),
                                 "gate": (slice(0, P), W, lx[:, 1, :])}[job[0]]
                pe.wait_ge(lora_in, 16)
                pe.wait_ge(lora_act, 2)
                b = begin(job)
                end(job, mm(b[:, 0:T], loraW[rows, c0 + p * P:c0 + (p + 1) * P], rhs, start=True, stop=True))

            def j_headsum(job, p):
                pe.wait_ge(kk_sq if job[0] == "ss" else rk_done, 1)
                b = begin(job)
                end(job, mm(b[:, 0:T], C("blk"), F_E[:, p, :], start=True, stop=True))

            def j_nat(job, tt, a):
                pe.wait_ge(tilde, 1)
                b = begin(job)
                for p in range(4):
                    i = tr(b[:, p * P:(p + 1) * P], (Vs, Zs, Bs, Ks)[a][:, p, cols(tt)], ident)
                end(job, i)

            def j_A(job, tt, hg, k):
                pe.wait_ge(tilde, 1)
                l, r = ((Bs, Zs), (Zs, Bs), (Ks, Zs), (Bs, Rs), (Ks, Rs))[k]
                r0 = hg * 64
                b = begin(job)
                for n in range(4):
                    i = mm(b[:, n * P:(n + 1) * P], l[r0:r0 + 64, n, cols(tt)], r[r0:r0 + 64, n, cols(tt)],
                           start=True, stop=True)
                end(job, i)

            def j_P(job, tt, lvl, hg):
                pe.wait_ge(lvl_mask, 10 * tt + 2 * (lvl - 1) + hg + 1)
                pe.wait_ge(x_init, 2 * tt + hg + 1)
                if lvl > 1:
                    evacuated(pe, ("XP", tt, lvl - 1, hg))
                b = begin(job)
                for n in range(4):
                    h = 4 * hg + n
                    i = mm(b[:, n * P:(n + 1) * P], MTl[:, h, :], X[:, h, :], start=True, stop=True)
                end(job, i)

            def j_XP(job, tt, lvl, hg):
                evacuated(pe, ("P", tt, lvl, hg))
                if lvl > 1:
                    evacuated(pe, ("XPT", tt, lvl - 1, hg))
                b = begin(job)
                for n in range(4):
                    h = 4 * hg + n
                    l, r = (XT[:, h, :], PM[:, h, :]) if job[0] == "XP" else (PM[:, h, :], XT[:, h, :])
                    i = mm(b[:, n * P:(n + 1) * P], l, r, start=True, stop=True)
                end(job, i)

            def j_G(job, tt):
                evacuated(pe, ("nat", tt, 0))
                evacuated(pe, ("A", tt, 0, 2)); evacuated(pe, ("A", tt, 1, 2))
                b = begin(job)
                for h in range(NH):
                    i = mm(b[:, h * 64:h * 64 + 64], AzkT[:, slot(h), :], nat[:, 0, h * 64:h * 64 + 64], start=True, stop=True)
                end(job, i)

            def j_U0(job, tt):
                evacuated(pe, ("XPT", tt, 5, 0)); evacuated(pe, ("XPT", tt, 5, 1)); evacuated(pe, ("G", tt))
                b = begin(job)
                for h in range(NH):
                    i = mm(b[:, h * 64:h * 64 + 64], XT[:, slot(h), :], Gn[:, h * 64:h * 64 + 64], start=True, stop=True)
                end(job, i)

            def j_TZ(job, tt, hf):
                evacuated(pe, ("nat", tt, 1))
                b = begin(job)
                for n in range(4):
                    h = 4 * hf + n
                    i = mm(b[:, n * P:(n + 1) * P], nat[:, 1, (h // 2) * P:(h // 2 + 1) * P], XT[:, slot(h), :],
                           start=True, stop=True)
                end(job, i)

            def j_U(job, c):
                evacuated(pe, ("TZ", c // 2, 0)); evacuated(pe, ("TZ", c // 2, 1))
                pe.wait_ge(state_ready, c + 1)
                b = begin(job)
                for p in range(4):
                    i = mm(b[:, p * P:(p + 1) * P], TZT[:, p, :], SBD[:, p, :], start=True, stop=True)
                end(job, i)

            def j_ys(job, c):
                b = begin(job)
                for p in range(4):
                    i = mm(b[:, p * CHUNK:(p + 1) * CHUNK], SBD[:, p, :], Rs[:, p, c * CHUNK:(c + 1) * CHUNK],
                           start=True, stop=True)
                end(job, i)

            def j_dS(job, c):
                rows = slice((c % 2) * 64, (c % 2) * 64 + 64)
                evacuated(pe, ("U", c))
                evacuated(pe, ("nat", c // 2, 2)); evacuated(pe, ("nat", c // 2, 3))
                b = begin(job)
                for p in range(4):
                    pc = slice(p * P, (p + 1) * P)
                    mm(b[:, pc], nat[rows, 2, pc], Un[rows, pc], start=True, stop=False)
                    i = mm(b[:, pc], nat[rows, 3, pc], nat[rows, 0, pc], start=False, stop=True)
                end(job, i)

            def j_yi(job, tt, hf):
                for hg in range(2):
                    evacuated(pe, ("A", tt, hg, 3)); evacuated(pe, ("A", tt, hg, 4))
                b = begin(job)
                for n in range(4):
                    h = 4 * hf + n
                    pc = slice((h // 2) * P, (h // 2 + 1) * P)
                    mm(b[:, n * P:(n + 1) * P], Un[:, pc], ArbT[:, slot(h), :], start=True, stop=False)
                    i = mm(b[:, n * P:(n + 1) * P], nat[:, 0, pc], ArkT[:, slot(h), :], start=False, stop=True)
                end(job, i)

            def j_Sout(job):
                pe.wait_ge(state_ready, 5)
                b = begin(job)
                for p in range(4):
                    i = tr(b[:, p * P:(p + 1) * P], SBD[:, p, :], ident)
                end(job, i)

            def j_sE(job, k, i):
                pe.wait_ge(sst_ready, 4 * k + i + 1)
                b = begin(job)
                end(job, mm(b[:, :], C("blk"), St[:, i, :, :].rearrange("p a b -> p (a b)"), start=True, stop=True))

            def j_PTs(job, hf):
                pe.wait_ge(s_prob, 1)
                b = begin(job)
                for j in range(8):
                    i = tr(b[:, j * 64:(j + 1) * 64], sc_s[0:64, (8 * hf + j) * P:(8 * hf + j + 1) * P], ident[0:64, 0:64])
                end(job, i)

            def j_poD(job):
                b = begin(job)
                end(job, mm(b[0:NB, 0:64], C("own8", NB, 64), g64b[:, :], start=True, stop=True))

            def j_OT(job):
                pe.wait_ge(o_copied, NB)
                bk = begin(job)
                for b in range(NB):
                    for c in range(4):
                        o = (c * NB + b) * 2
                        i = mm(bk[:, o:o + 2], OmS(b)[:, c * P:(c + 1) * P], ident[0:NH, 2 * c:2 * c + 2],
                               start=True, stop=True)
                end(job, i)

            def j_stat(job, t):
                n = tok[t][1]
                if job[0] == "mean":
                    pe.wait_ge(y_done[t], 1)
                else:
                    pe.wait_ge(ysq_ready, t + 1)
                b = begin(job)
                for p in range(4):
                    src = F_y[:, p, cols(t)] if job[0] == "mean" else tmpY[:, p * n:(p + 1) * n]
                    i = mm(b[:, p * n:(p + 1) * n], C("blk"), src, start=True, stop=True)
                end(job, i)

            def j_h(job, t, hf):
                t0, n = tok[t]
                pe.wait_ge(cat_ready, t + 1)
                b = begin(job)
                end(job, project(b, n, lambda c: cat[:, c, t0:t0 + n], H_LOAD[min(t, 1)] + 2 * hf))

            def j_xfT(job, t, h):
                n = tok[t][1]
                pe.wait_ge(xf_ready, t + 1)
                b = begin(job)
                for c in range(4):
                    i = tr(b[:, c * P:c * P + n], xf[0:n, t, (4 * h + c) * P:(4 * h + c + 1) * P], ident[0:n, 0:n])
                end(job, i)

            def j_qT(job, g, j):
                t0, n, ts = grp[g]
                if j == 0:
                    for t in ts:
                        evacuated(pe, ("xfT", t, 0)); evacuated(pe, ("xfT", t, 1))
                load = Q_LOAD[g] + j
                w_arrived(pe, load)
                b = begin(job)
                for k in range(2):
                    for c in range(KC):
                        i = mm(b[:, k * n:(k + 1) * n], wslot[W_SLOT[load]][:, c, k * P:(k + 1) * P], xfTg(g)[:, c, :],
                               start=(c == 0), stop=(c == KC - 1))
                end(job, i)

            def j_sc(job, t, q):
                g = min(t, 1)
                n, gn = tok[t][1], grp[g][1]
                o = tok[t][0] - grp[g][0]
                pe.wait_ge(subk_in, 16)
                evacuated(pe, ("qT", g, 2 * q)); evacuated(pe, ("qT", g, 2 * q + 1))
                b = begin(job)
                for k in range(4):
                    hp = 4 * q + k
                    i = mm(b[0:n, k * P:(k + 1) * P], qT[:, hp * gn + o:hp * gn + o + n], subk[:, hp % 2, :],
                           start=True, stop=True)
                end(job, i)

            def j_jT(job):
                pe.wait_ge(routed, 3)
                b = begin(job)
                tr(b[:, 0:NB], idxf[0:NB, :], ident[0:NB, 0:NB])
                end(job, tr(b[:, NB:2 * NB], gateS[:, :], ident[0:NB, 0:NB]))

            def j_xb(job, b, hf):
                pe.wait_ge(sel8_in, 16)
                bk = begin(job)
                end(job, mm(bk[:, :], sel8[:, b * P:(b + 1) * P], xf[0:NB, 2, hf * 512:(hf + 1) * 512],
                            start=True, stop=True))

            do = {"xT": j_xT, "pT": j_pT, "qkv": j_qkv, "qkT": j_qkT, "own": j_own, "S": j_S, "PT": j_PT, "PV": j_PV,
                  "dec": j_lora, "aaa": j_lora, "gate": j_lora, "ss": j_headsum, "bon": j_headsum, "nat": j_nat,
                  "A": j_A, "P": j_P, "XP": j_XP, "XPT": j_XP, "G": j_G, "U0": j_U0, "TZ": j_TZ, "U": j_U, "ys": j_ys,
                  "dS": j_dS, "yi": j_yi, "Sout": j_Sout, "sE": j_sE, "PTs": j_PTs, "poD": j_poD, "OT": j_OT,
                  "mean": j_stat, "var": j_stat, "h": j_h, "xfT": j_xfT, "qT": j_qT, "sc": j_sc, "jT": j_jT, "xb": j_xb}
            pe.wait_ge(const_in, 16)
            for x in order:
                if x[0] == "cache":
                    half_unit(x[1], x[2])
                elif x[0] == "v":
                    t, rd = x[1:]
                    value_rows(t, 16 * (rd + uses_before(t, 1, rd) + 1), len(SHARE) * shared_round(t, rd) + 1,
                               start=rd == (SHARED0 if t == 0 else 0), stop=(t, rd) == (0, 15))
                else:
                    do[x[0]](x, *x[1:])
            samples_rows()
            with pe.Fori(10, 15) as rd:
                value_rows(1, rd * 16 + 16 * (uses_before(1, 1, 10) + 1),
                           rd * len(SHARE) + (len(SHARE) * shared_round(1, 0) + 1))
            value_rows(1, 16 * (uses_before(1, 1, 15) + 16), len(SHARE) * shared_round(1, 15) + 1, stop=True)

        @block.scalar
        def _(act):
            ch = Chain(act, act_step)

            def rms(src, scratch, dst, done):
                n = src.shape[0]
                ch.link(ta.activation(scratch, src, ACT.Square, scale=D_MODEL ** -0.5, accum_out=dst))
                ta.activation(dst, dst, ACT.Sqrt, bias=C("eps", 1, n)).then_inc(done, 1)

            def diagonals(use, k):
                act.wait_ge(w8_ready, k + 1)
                for n, s in enumerate(SHARE):
                    act.wait_ge(row_used[s], use)
                    ta.activation(diag[:, n, :], ident, ACT.Copy, scale=w8[:, s:s + 1]).then_inc(diag_ready, 1)

            def copy(dst, src, job):
                filled(act, job)
                empties(ta.activation(dst, src, ACT.Copy), job)

            def gate_exp(t):
                g_ = gate[:, t, :] if t < 2 else gateS[:, :]
                act.wait_ge(cs_ready, t + 1)
                ta.activation(g_, g_, ACT.Exp).then_inc(g_exp, 1)

            act.wait_ge(const_in, 16)
            for t, (t0, n) in enumerate(tok):
                act.wait_ge(x_in[t], 16)
                rms(xn[0:n, t, :], hx[0:n, 5120:6144], st4[0:n, t:t + 1], xsq)
            for x in order:
                k, a = x[0], x[1:]
                if x == ("dec", 0):
                    act.wait_ge(shifted, 1)
                    ta.activation(lx[0:64, 0, :], lx[0:64, 0, :], ACT.Tanh).then_inc(lora_act, 1)
                    ta.activation(lx[:, 1, :], lx[:, 1, :], ACT.Sigmoid).then_inc(lora_act, 1)
                if x == ("qkT", 0, 0):
                    act.wait_ge(cum_ready, 1)
                    ta.activation(WC[:, :, :], F_C[:, :, CHUNK - 1:SEQ:CHUNK], ACT.Exp)
                    ta.activation(sw[:, :, :], F_logw[:, :, SEQ:T], ACT.Exp)
                    ta.activation(F_E[:, :, 0:SEQ], F_E[:, :, 0:SEQ], ACT.Exp).then_inc(exp1, 1)
                    act.wait_ge(cum_ready, 2)
                    ta.activation(F_logw[:, :, 0:SEQ], F_C[:, :, 0:SEQ], ACT.Exp, scale=-1.0)
                    ta.activation(F_E[:, :, 0:SEQ], F_C[:, :, 0:SEQ], ACT.Exp).then_inc(exp2, 1)
                if k == "PT":
                    act.wait_ge(att_masked, a[0] + 1)
                    nh = 4 if a[0] < 2 else 2
                    flat = att_s.rearrange("p a b -> p (a b)")
                    w = 512 // nh
                    for n in range(nh):
                        i = ta.activation(flat[:, n * w:(n + 1) * w], flat[:, n * w:(n + 1) * w], ACT.Exp,
                                          bias=st4[:, 4 + n:5 + n], scale=SCALE, accum_out=st4[:, 8 + n:9 + n])
                    i.then_inc(att_exp, 1)
                if x == ("PTs", 0):
                    act.wait_ge(s_max, 1)
                    ta.activation(sc_s[0:64, :], sc_s[0:64, :], ACT.Exp, bias=g64[:, 33:34], scale=SCALE,
                                  accum_out=g64[:, 34:35])
                    ta.activation(g64[:, 35:36], g64[:, 32:33], ACT.Exp, bias=g64[:, 33:34], scale=SCALE).then_inc(s_exp, 1)
                if x == ("TZ", 1, 0):
                    act.wait_ge(u_done, 1)
                    ta.activation(actv[:, :], actv[:, :], ACT.Gelu).then_inc(gelu_done, 1)
                if x == ("xfT", 0, 0):
                    act.wait_ge(h_ready, 1)
                    rms(hb[:, 0, :], xf[:, 0, :], st4[:, 0:1], h_sq)
                if x == ("xfT", 1, 0):
                    for t in (1, 2):
                        act.wait_ge(h_ready, t + 1)
                        rms(hb[0:tok[t][1], t, :], xf[0:tok[t][1], t, :], st4[0:tok[t][1], t:t + 1], h_sq)
                if k == "pT":
                    copy(pT[:, a[0], 1:T + 1], bank(x)[:, 0:T], x)
                elif k == "qkv":
                    n = tok[a[1]][1]
                    dst = stage[0:n, a[1], a[0] * W:(a[0] + 1) * W] if a[0] < 2 else vN[0:n, a[1], :]
                    copy(dst, bank(x)[0:n, :], x)
                elif k == "PT":
                    copy(att_t.rearrange("p a b -> p (a b)"), bank(x)[:, :], x)
                elif k in ("dec", "aaa"):
                    dst, bias = (F_logw, "w0") if k == "dec" else (F_a, "a0")
                    filled(act, x)
                    empties(ta.activation(dst[:, a[0], :], bank(x)[:, 0:T], ACT.Sigmoid,
                                          bias=prmv(bias)[:, a[0]:a[0] + 1]), x)
                elif k == "gate":
                    copy(F_g[:, a[0], :], bank(x)[:, 0:T], x)
                elif k == "ss" and a[0] == 3:
                    for p in range(4):
                        evacuated(act, ("ss", p))
                    ta.activation(F_C[:, :, :], F_C[:, :, :], ACT.Sqrt).then_inc(kk_norm, 1)
                elif k == "nat":
                    copy(nat[:, a[1], :], bank(x)[:, :], x)
                elif k == "P":
                    hg = a[2]
                    copy(PM[:, 4 * hg:4 * hg + 4, :].rearrange("p a b -> p (a b)"), bank(x)[:, :], x)
                elif k in ("G", "U0", "Sout"):
                    copy(Gn[:, :], bank(x)[:, :], x)
                    if k == "Sout":
                        evacuated(act, x)
                        act.sem_inc(sout_copied, 1)
                elif k == "TZ":
                    filled(act, x)
                    act.wait_ge(out_shift, 16)
                    bv = bank(x)[:, :].rearrange("p (a r t) -> p a r t", a=2, r=2)
                    hf = a[1]
                    ta.activation(TZT[0:64, 2 * hf:2 * hf + 2, :], bv[0:64, :, 0, :], ACT.Copy)
                    empties(ta.activation(TZT[64:128, 2 * hf:2 * hf + 2, :], bv[64:128, :, 1, :], ACT.Copy), x)
                elif k == "ys":
                    c = a[0]
                    copy(F_y[:, :, c * CHUNK:(c + 1) * CHUNK], bank4(x, CHUNK), x)
                elif k == "PTs":
                    copy(PTs[:, 8 * a[0]:8 * a[0] + 8, :].rearrange("p a b -> p (a b)"), bank(x)[:, :], x)
                elif k == "poD":
                    copy(small[:, :], bank(x)[0:NB, 0:64], x)
                elif k == "cache" and a[0] >= 32 and a[0] % 4 == 3 and a[1] == 1:
                    b = (a[0] - 32) // 4
                    act.wait_ge(o_done, b + 1)
                    if b == 0:
                        for t in range(3):
                            act.wait_ge(out_kv[t], 32)
                    ta.activation(OmS(b), pS[0:NH, (b % 4) * 512:(b % 4 + 1) * 512], ACT.Copy).then_inc(o_copied, 1)
                elif k == "v":
                    t, rd = a
                    diagonals(rd + uses_before(t, 1, rd), shared_round(t, rd))
                elif k == "var":
                    act.wait_ge(gn_var, a[0] + 1)
                    n4 = 4 * tok[a[0]][1]
                    ta.activation(tmpY[:, 0:n4], tmpY[:, 0:n4], ACT.Sqrt).then_inc(gn_std, 1)
                elif k == "qT":
                    g, j = a
                    n = grp[g][1]
                    copy(qT[:, 2 * j * n:(2 * j + 2) * n], bank(x)[:, 0:2 * n], x)
                if x == ("sc", 0, 3):
                    gate_exp(0)
                if x == ("v", 0, 14):
                    gate_exp(1)
                if x == ("v", 0, 15):
                    act.wait_ge(acc_ready, 1)
                    rms(hb[:, 0, :], xf[:, 0, :], st4[:, 12:13], y_sq)
                    act.wait_ge(u_done, 2)
                    ta.activation(actv[:, :], actv[:, :], ACT.Gelu).then_inc(gelu_done, 1)
                if x == ("v", 1, 5):
                    gate_exp(2)
                if x == ("xb", NB - 1, 1):
                    act.wait_ge(u_done, 3)
                    ta.activation(actS[:], actS[:], ACT.Gelu).then_inc(gelu_done, 1)
            def final_rms(n, t):
                act.wait_ge(acc_ready, n)
                rows = slice(0, tok[t][1])
                rms(hb[rows, t, :], xf[rows, t, :], st4[rows, 12:13], y_sq)

            with act.Fori(10, 12) as rd:
                diagonals(rd + uses_before(1, 1, 10), rd + shared_round(1, 0))
            final_rms(2, 2)
            with act.Fori(12, 16) as rd:
                diagonals(rd + uses_before(1, 1, 10), rd + shared_round(1, 0))
            final_rms(3, 1)

        @block.gpsimd
        def _(pool):
            def masks(tt):
                for lvl in range(1, 6):
                    for hg in range(2):
                        hs = slice(4 * hg, 4 * hg + 4)
                        pool.wait_ge(x_init, 2 * tt + hg + 1)
                        if lvl > 1:
                            filled(pool, ("P", tt, lvl - 1, hg))
                        tg.tensor_tensor(MTl[:, hs, :], MT[:, hs, :],
                                         bc(C(f"lvl{lvl}U").unsqueeze(1), P, 4, P), ALU.mult).then_inc(lvl_mask, 1)

            def gathers(t, kind, i, q0, first, moved=0):
                table = A["expert_u"] if kind == 0 else A["expert_v"]
                for par in range(2):
                    for s in range(RS):
                        if not (first and par == 0):
                            pool.wait_ge(row_used[s], i * 2 + (q0 + par))
                            pool.sem_inc(slot_open, 1)
                        if s == 0:
                            tg.tensor_copy(idxh[:, par, :], idx[:, t, bass.ds(i * 2 * RS + par * RS, RS)])\
                                .then_inc(idx_moved, 1)
                            pool.wait_ge(idx_moved, i * 2 + (q0 + par + 1 - moved))
                            pool.sem_inc(slot_open, 1)
                        tg.indirect_dma_start(ring[:, s, :], None, table,
                                              bass.IndirectOffsetOnAxis(ap=idxh[:, par, s:s + 1], axis=0))\
                            .then_inc(gathered[s], 16)

            pool.wait_ge(const_in, 16)
            masks(0)
            pool.wait_ge(routed, 1)
            filled(pool, ("qT", 0, 7))
            gathers(0, 0, 0, 0, True)
            with pool.Fori(1, PEER_H) as i:
                gathers(0, 0, i, 0, False)
            with pool.Fori(0, PEER_H) as i:
                gathers(0, 1, i, 16, False)
            pool.wait_ge(routed, 2)
            with pool.Fori(0, PEER_H) as i:
                gathers(1, 0, i, 32, False)
            def samples(table, use):
                for b in range(NB):
                    pool.wait_ge(row_used[b], use)
                    tg.indirect_dma_start(ring[:, b, :], None, table,
                                          bass.IndirectOffsetOnAxis(ap=idxTs[:, b:b + 1], axis=0))\
                        .then_inc(gathered[b], 16)

            with pool.Fori(0, 4) as i:
                gathers(1, 1, i, 48, False)
            pool.wait_ge(sT_ready, 1)
            samples(A["expert_u"], 56)
            gathers(1, 1, 4, 49, False, 1)
            samples(A["expert_v"], 59)
            with pool.Fori(5, PEER_H) as i:
                gathers(1, 1, i, 50, False, 2)

        @block.vector
        def _(dve):
            ch = Chain(dve, dve_step)
            L = ch.link
            tt_, ts_, stt = tv.tensor_tensor, tv.tensor_scalar, tv.scalar_tensor_tensor

            def mask4(name):
                return bc(C(name).unsqueeze(1), P, 4, P)

            L(tv.memset(pT[:, :, 0:1], 0.0))
            dve.wait_ge(const_in, 16)
            dve.wait_ge(prm_in, 16)
            for t, (t0, n) in enumerate(tok):
                dve.wait_ge(xsq, t + 1)
                L(tv.reciprocal(st4[0:n, t:t + 1], st4[0:n, t:t + 1]))
                ts_(xn[0:n, t, :], xn[0:n, t, :], st4[0:n, t:t + 1], None, ALU.mult).then_inc(xnorm, 1)
            for t, (t0, n) in enumerate(tok):
                for h in range(2):
                    filled(dve, ("xT", t, h))
                    b = bank(("xT", t, h))[:, :].rearrange("p (c n) -> p c n", c=4)[:, :, 0:n]
                    i = tt_(xT[:, 4 * h:4 * h + 4, t0:t0 + n], b,
                            bc(prmv("norm_mix")[:, 4 * h:4 * h + 4].unsqueeze(2), P, 4, n), ALU.mult)
                    empties(i, ("xT", t, h))
            dve.wait_ge(shift_in, 16)
            for f in [12, 13] + list(range(12)):
                dst = ps[:, f, :] if f < 12 else lx[:, f - 12, :]
                evacuated(dve, ("pT", f))
                tt_(dst[:, 0:SEQ], pT[:, f, 0:SEQ], pT[:, f, 1:SEQ + 1], ALU.subtract)
                L(tt_(dst[:, SEQ:T], Un[:, f * NB:(f + 1) * NB], pT[:, f, SEQ + 1:T + 1], ALU.subtract))
                i = stt(dst, dst, prmv("mu")[:, f:f + 1], pT[:, f, 1:T + 1], ALU.mult, ALU.add)
                if f == 13:
                    i.then_inc(shifted, 1)
            L(i)
            tv.tensor_copy(shout, pT[:, :, SEQ:T + 1]).then_inc(shift_out_ready, 1)
            dve.wait_ge(shift_out_ready, 1)
            kraw, r, v = ps[:, 4:8, :], ps[:, 0:4, :], ps[:, 8:12, :]
            L(tt_(F_kk[:], kraw, bc(prmv("k_k").unsqueeze(2), P, 4, T), ALU.mult))
            tt_(F_E, F_kk[:], F_kk[:], ALU.mult).then_inc(kk_sq, 1)
            for p in range(4):
                evacuated(dve, ("dec", p))
            L(ts_(F_logw, F_logw, -EXPM05, None, ALU.mult))
            for p in range(4):
                filled(dve, ("ss", p))
                empties(ts_(F_C[:, p, :], bank(("ss", p))[:, 0:T], 1e-24, None, ALU.max), ("ss", p))
            dve.wait_ge(kk_norm, 1)
            L(tv.reciprocal(F_C[:], F_C[:]))
            L(tt_(F_kk[:], F_kk[:], F_C[:], ALU.mult))
            for p in range(4):
                evacuated(dve, ("aaa", p))
            for p in range(4):
                i = ts_(F_C[:, p, :], F_a[:, p, :], 1.0, prmv("k_a")[:, p:p + 1], ALU.subtract, ALU.mult)
            L(i)
            L(stt(kraw, F_C[:], 1.0, kraw, ALU.add, ALU.mult))
            L(tt_(F_a[:], F_kk[:], F_a[:], ALU.mult))
            for p in range(4):
                i = stt(F_E[:, p, :], r[:, p, :], prmv("r_k")[:, p:p + 1], kraw[:, p, :], ALU.mult, ALU.mult)
            i.then_inc(rk_done, 1)

            def rope(t):
                n = tok[t][1]
                for part in range(3):
                    evacuated(dve, ("qkv", part, t))
                src = stage[0:n, t, :].rearrange("p (h d) -> p h d", d=DH)
                tab = C("rope", 32)[:, 16 * t:16 * t + 16] if t < 2 else C("rope_s", 16, NB)
                cos, sin = [bc(tab[:, k:k + 8].unsqueeze(1), n, 16, 8) for k in (0, 8)]
                x1, x2 = src[:, :, 0:8], src[:, :, 8:16]
                q = [r16[0:n, k] for k in range(4)]
                tt_(q[0], x1, cos, ALU.mult)
                tt_(q[1], x2, sin, ALU.mult)
                tt_(q[2], x2, cos, ALU.mult)
                L(tt_(q[3], x1, sin, ALU.mult))
                tt_(x1, q[0], q[1], ALU.subtract)
                tt_(x2, q[2], q[3], ALU.add).then_inc(roped[t], 1)
                dve.wait_ge(roped[t], 1)

            def qkT_copy(t):
                t0, n = tok[t]
                for w in range(2):
                    job = ("qkT", t, w)
                    filled(dve, job)
                    empties(tv.tensor_copy(qkT[:, 4 * w:4 * w + 4, t0:t0 + n], bank4(job)[:, :, 0:n]), job)

            rope(0)
            for p in range(4):
                filled(dve, ("bon", p))
                i = tt_(F_bonus[:, p, :], bank(("bon", p))[:, 0:T], v[:, p, :], ALU.mult)
                empties(i, ("bon", p))
            evacuated(dve, ("bon", 3))
            for p in range(4):
                i = tv.tensor_tensor_scan(F_C[:, p, 0:SEQ], C("scan", SEQ), F_logw[:, p, 0:SEQ], 0.0, ALU.mult, ALU.add)
            L(i)
            tt_(F_E[:, :, 0:SEQ], F_C[:, :, 0:SEQ], F_logw[:, :, 0:SEQ], ALU.subtract).then_inc(cum_ready, 1)
            dve.wait_ge(exp1, 1)
            pr = slice(0, SEQ)
            L(stt(F_kk[:, :, pr], F_kk[:, :, pr], -1.0, F_E[:, :, pr], ALU.mult, ALU.mult))
            dve.sem_inc(cum_ready, 1)
            dve.wait_ge(exp2, 1)
            tt_(F_a[:, :, pr], F_a[:, :, pr], F_logw[:, :, pr], ALU.mult)
            tt_(kraw[:, :, pr], kraw[:, :, pr], F_logw[:, :, pr], ALU.mult)
            tt_(r[:, :, pr], r[:, :, pr], F_E[:, :, pr], ALU.mult).then_inc(tilde, 1)
            tv.memset(SBD[:], 0.0).then_inc(state_ready, 1)
            dve.wait_ge(tilde, 1)
            L(tv.memset(Qz, 0.0))
            rope(2)
            qkT_copy(0)
            qkT_copy(2)
            evacuated(dve, ("qkT", 2, 0))
            for c in range(4):
                for par in range(2):
                    r0 = par * 64
                    o = 2 * c + par
                    z = Qz[r0:r0 + 64, c, :, :].rearrange("p b x -> p (b x)")
                    i = tv.tensor_copy(z[:, o:o + 72 * 7 + 1:72], qkT[r0:r0 + 64, c, SEQ:T])
            i.then_inc(q_spread, 1)

            def a_matrices(tt, kinds):
                for hg in range(2):
                    hs = slice(4 * hg, 4 * hg + 4)
                    for k in kinds:
                        job = ("A", tt, hg, k)
                        filled(dve, job)
                        if k == 1:
                            empties(tt_(X[:, hs, :], bank4(job), mask4("lvl0L"), ALU.mult), job)
                            evacuated(dve, job)
                            L(tt_(X[:, hs, :], X[:, hs, :], mask4("ident"), ALU.add))
                            dve.sem_inc(x_init, 1)
                            continue
                        dst, m = {0: (MT, "strictU"), 2: (AzkT, "strictU"), 3: (ArbT, "inclU"), 4: (ArkT, "inclU")}[k]
                        empties(tt_(dst[:, hs, :], bank4(job), mask4(m), ALU.mult), job)
                        if k == 0:
                            evacuated(dve, job)
                            L(tt_(XT[:, hs, :], MT[:, hs, :], mask4("lvl0U"), ALU.mult))
                            L(tt_(XT[:, hs, :], XT[:, hs, :], mask4("ident"), ALU.add))

            def level_masks(lvl):
                for hg in range(2):
                    hs = slice(4 * hg, 4 * hg + 4)
                    if lvl > 1:
                        filled(dve, ("P", 1, lvl - 1, hg))
                    tt_(MTl[:, hs, :], MT[:, hs, :], mask4(f"lvl{lvl}U"), ALU.mult).then_inc(lvl_mask, 1)

            def level(tt, lvl):
                for hg in range(2):
                    hs = slice(4 * hg, 4 * hg + 4)
                    for k, dst in (("XP", X), ("XPT", XT)):
                        filled(dve, (k, tt, lvl, hg))
                        if lvl > 1:
                            evacuated(dve, (k, tt, lvl - 1, hg))
                        empties(tt_(dst[:, hs, :], dst[:, hs, :], bank4((k, tt, lvl, hg)), ALU.add), (k, tt, lvl, hg))

            def chunk(c):
                evacuated(dve, ("U0", c // 2))
                rows = slice((c % 2) * 64, (c % 2) * 64 + 64)
                filled(dve, ("U", c))
                empties(tt_(Un[rows, :], bank(("U", c))[rows, :], Gn[rows, :], ALU.add), ("U", c))
                filled(dve, ("dS", c))
                empties(tt_(tmpY4, bank4(("dS", c)), mask4("blk"), ALU.mult), ("dS", c))
                evacuated(dve, ("dS", c))
                L(tt_(SBD[:], SBD[:], tmpY4, ALU.add))
                tt_(SBD[:], SBD[:], bc(WC[:, :, c:c + 1], P, 4, P), ALU.mult).then_inc(state_ready, 1)
                dve.wait_ge(state_ready, c + 2)

            def y_inner(tt):
                for c in (2 * tt, 2 * tt + 1):
                    evacuated(dve, ("ys", c))
                for hf in range(2):
                    job = ("yi", tt, hf)
                    filled(dve, job)
                    bv = bank(job)[:, :].rearrange("p (a r t) -> p a r t", a=2, r=2)
                    for par in range(2):
                        rw = slice(par * 64, par * 64 + 64)
                        y = F_y[rw, 2 * hf:2 * hf + 2, tt * P:(tt + 1) * P]
                        i = tt_(y, y, bv[rw, :, par, :], ALU.add)
                    empties(i, job)
                evacuated(dve, ("yi", tt, 1))
                dve.sem_inc(y_done[tt], 1)

            def y_post(t):
                n = tok[t][1]
                y, tmp = F_y[:, :, cols(t)], grid(tmpY, 0, 4, n)
                filled(dve, ("mean", t))
                empties(stt(y, bank4(("mean", t), n), -1.0 / DH, y, ALU.mult, ALU.add), ("mean", t))
                evacuated(dve, ("mean", t))
                tt_(tmp, y, y, ALU.mult).then_inc(ysq_ready, 1)
                filled(dve, ("var", t))
                empties(ts_(tmp, bank4(("var", t), n), 1.0 / DH, GN_EPS, ALU.mult, ALU.add), ("var", t))
                evacuated(dve, ("var", t))
                dve.sem_inc(gn_var, 1)
                dve.wait_ge(gn_std, t + 1)
                L(tv.reciprocal(tmp, tmp))
                L(tt_(y, y, tmp, ALU.mult))
                L(tt_(y, y, bc(prmv("gn_g").unsqueeze(2), P, 4, n), ALU.mult))
                L(tt_(y, y, bc(prmv("gn_b").unsqueeze(2), P, 4, n), ALU.add))
                L(tt_(y, y, F_bonus[:, :, cols(t)], ALU.add))
                tt_(cat[:, 0:4, cols(t)], y, F_g[:, :, cols(t)], ALU.mult).then_inc(cat_ready, 1)

            def att_a(u):
                nh = 4 if u < 2 else 2
                job = ("S", u)
                filled(dve, job)
                if u < 2:
                    i = tt_(att_s, bank4(job), mask4("causal"), ALU.add)
                else:
                    bv = bank4(job).rearrange("p (h k) t -> p h k t", k=2)
                    av = att_s.rearrange("p (h k) t -> p h k t", k=2)
                    tv.tensor_copy(av[:, :, 0, :], bv[:, :, 0, :])
                    i = tt_(av[:, :, 1, :], bv[:, :, 1, :], bc(C("causal").unsqueeze(1), P, 2, P), ALU.add)
                empties(i, job)
                evacuated(dve, job)
                flat = att_s.rearrange("p a b -> p (a b)").rearrange("p (h w) -> p h w", h=nh)
                L(tv.reduce_max(st4[:, 4:4 + nh], flat, axis=AX))
                ts_(st4[:, 4:4 + nh], st4[:, 4:4 + nh], -SCALE, None, ALU.mult).then_inc(att_masked, 1)

            def att_b(u):
                nh = 4 if u < 2 else 2
                flat = att_s.rearrange("p a b -> p (a b)").rearrange("p (h w) -> p h w", h=nh)
                dve.wait_ge(att_exp, u + 1)
                L(tv.reciprocal(st4[:, 8:8 + nh], st4[:, 8:8 + nh]))
                if u:
                    filled(dve, ("PT", u - 1))
                else:
                    dve.wait_ge(out_shift, 16)
                tt_(att_p.rearrange("p a b -> p (a b)").rearrange("p (h w) -> p h w", h=nh), flat,
                    bc(st4[:, 8:8 + nh].unsqueeze(2), P, nh, 512 // nh), ALU.mult).then_inc(att_norm, 1)
                dve.wait_ge(att_norm, u + 1)

            def att_c(u):
                filled(dve, ("PV", u))
                for n in range(4 if u < 2 else 2):
                    h = unit(u)[n if u < 2 else 2 * n][0]
                    r0 = (h % 2) * 64
                    q0 = 0 if u < 2 else P
                    i = tv.tensor_copy(cat[r0:r0 + 64, 4 + h // 2, q0:q0 + P], bank(("PV", u))[r0:r0 + 64, n * P:(n + 1) * P])
                empties(i, ("PV", u))

            def residual(t, hf):
                n = tok[t][1]
                job = ("h", t, hf)
                filled(dve, job)
                dve.wait_ge(x2_in[t], 16)
                part = slice(hf * 512, (hf + 1) * 512)
                empties(tt_(hb[0:n, t, part], hb[0:n, t, part], bank(job)[0:n, :], ALU.add), job)
                if hf == 1:
                    evacuated(dve, job)
                    dve.sem_inc(h_ready, 1)

            def norm(t):
                n = tok[t][1]
                dve.wait_ge(gain_in, 16)
                dve.wait_ge(h_sq, t + 1)
                L(tv.reciprocal(st4[0:n, t:t + 1], st4[0:n, t:t + 1]))
                stt(xf[0:n, t, :], hb[0:n, t, :], st4[0:n, t:t + 1], gain[0:n, :], ALU.mult, ALU.mult).then_inc(xf_ready, 1)

            def xfT_copy(t):
                g = min(t, 1)
                o, n = tok[t][0] - grp[g][0], tok[t][1]
                for h in range(2):
                    job = ("xfT", t, h)
                    filled(dve, job)
                    empties(tv.tensor_copy(xfTg(g)[:, 4 * h:4 * h + 4, o:o + n], bank4(job)[:, :, 0:n]), job)

            def top16(n, src, val, ind, job=None):
                w = src[0].shape[-1]
                for k in range(4):
                    i = tv.max(val[k][:, 0:8], src[k])
                L(i)
                for k in range(4):
                    tv.max_index(ind[k][:, 0:8], val[k][:, 0:8], src[k])
                for k in range(4):
                    i = tv.match_replace(work[0:n, k, 0:w], val[k][:, 0:8], src[k], -3.0e38)
                if job:
                    empties(i, job)
                    evacuated(dve, job)
                else:
                    L(i)
                for k in range(4):
                    i = tv.max(val[k][:, 8:16], work[0:n, k, 0:w])
                L(i)
                for k in range(4):
                    i = tv.max_index(ind[k][:, 8:16], val[k][:, 8:16], work[0:n, k, 0:w])
                L(i)

            def rank_halves(t, q):
                n = tok[t][1]
                R, job = slice(0, n), ("sc", t, q)
                filled(dve, job)
                top16(n, [bank(job)[R, k * P:(k + 1) * P] for k in range(4)], [sv[R, 4 * q + k, :] for k in range(4)],
                      [si_u[R, 4 * q + k, :] for k in range(4)], job)

            def rank_sums(t):
                n = tok[t][1]
                R = slice(0, n)
                if t == 1:
                    filled(dve, ("sc", 2, 3))
                L(tv.tensor_copy(sif[R], si_u[R]))
                svv = sv[R].rearrange("p (h k) a -> p h k a", k=2)
                c4 = comb[R].rearrange("p h (a b) -> p h a b", a=16)
                L(tt_(c4, bc(svv[:, :, 0, :].unsqueeze(3), n, 8, 16, 16), bc(svv[:, :, 1, :].unsqueeze(2), n, 8, 16, 16), ALU.add))
                civ = ci_u[R, :].rearrange("p (h k) -> p h k", h=8)
                for h in (0, 4):
                    top16(n, [comb[R, h + k, :] for k in range(4)], [cs[R, h + k, :] for k in range(4)],
                          [civ[:, h + k, :] for k in range(4)])

            def route(t):
                n = tok[t][1]
                R = slice(0, n)
                gv = (gate[R, t, :] if t < 2 else gateS[:, :]).rearrange("p (h k) -> p h k", h=8)
                tt_(gv, cs[R], bc(cs[R, :, 0:1], n, 8, 16), ALU.subtract).then_inc(cs_ready, 1)
                ts_(hi_u[R, :], ci_u[R, :], 4, None, ALU.logical_shift_right)
                L(ts_(ci_u[R, :], ci_u[R, :], 15, None, ALU.bitwise_and))
                tv.tensor_copy(ehi[R], hi_u[R, :])
                L(tv.tensor_copy(elo[R], ci_u[R, :]))
                siv = sif[R].rearrange("p (h k) a -> p h k a", k=2)
                oh4 = oh[R].rearrange("p (h k) a -> p h k a", h=8)
                for k, src, dst in ((0, ehi, e1), (1, elo, e2)):
                    L(tt_(oh[R], bc(src[R].unsqueeze(2), n, NJ, 16), bc(C("iota16", 16, n).unsqueeze(1), n, NJ, 16), ALU.is_equal))
                    L(tt_(oh4, oh4, bc(siv[:, :, k, :].unsqueeze(2), n, 8, 16, 16), ALU.mult))
                    L(tv.reduce_sum(dst[R], oh[R], axis=AX))
                L(stt(idxf[R], e1[R], float(NKEYS), e2[R], ALU.mult, ALU.add))
                if t < 2:
                    L(tv.tensor_copy(idx[:, t, :], idxf))
                    dve.sem_inc(routed, 1)
                dve.wait_ge(g_exp, t + 1)
                L(tv.reduce_sum(mx8[R, 0:8], gv, axis=AX))
                L(tv.reciprocal(mx8[R, 0:8], mx8[R, 0:8]))
                L(tt_(gv, gv, bc(mx8[R, 0:8].unsqueeze(2), n, 8, 16), ALU.mult))
                if t == 2:
                    dve.sem_inc(routed, 1)

            a_matrices(0, (0, 1, 2))
            att_a(0)
            level(0, 1)
            att_b(0)
            level(0, 2)
            att_c(0)
            att_a(1)
            level(0, 3)
            att_b(1)
            level(0, 4)
            att_c(1)
            level(0, 5)
            a_matrices(0, (3, 4))
            chunk(0)
            chunk(1)
            y_inner(0)
            y_post(0)
            residual(0, 0)
            residual(0, 1)
            rope(1)
            norm(0)
            qkT_copy(1)
            filled(dve, ("own",))
            empties(tv.tensor_copy(g64[:, 32:33], bank(("own",))[0:64, 0:1]), ("own",))
            xfT_copy(0)
            for q in range(4):
                rank_halves(0, q)
            rank_sums(0)
            route(0)

            def smp(region, i):
                return bc(region[:, i, SEQ:T].unsqueeze(2), P, NB, DH)

            def bank_s(job):
                return bank(job)[:, :].rearrange("p (b v) -> p b v", b=NB)

            dup = bc(C("dup64", DH).unsqueeze(1), P, NB, DH)

            def state_0():
                dve.wait_ge(state_in, 16)
                for i in range(4):
                    tt_(St[:, i], Ss[:, i], smp(F_kk, i), ALU.mult).then_inc(sst_ready, 1)

            def state_1():
                for i in range(4):
                    filled(dve, ("sE", 0, i))
                    empties(tt_(St[:, i], bank_s(("sE", 0, i)), smp(F_a, i), ALU.mult), ("sE", 0, i))
                    L(tt_(Ss[:, i], Ss[:, i], bc(sw[:, i, :].unsqueeze(2), P, NB, DH), ALU.mult))
                    evacuated(dve, ("sE", 0, i))
                    L(tt_(Ss[:, i], Ss[:, i], St[:, i], ALU.subtract))
                    tt_(St[:, i], dup, smp(Vs, i), ALU.mult).then_inc(sst_ready, 1)

            def state_2():
                for i in range(4):
                    filled(dve, ("sE", 1, i))
                    empties(tt_(St[:, i], bank_s(("sE", 1, i)), smp(Ks, i), ALU.mult), ("sE", 1, i))
                    evacuated(dve, ("sE", 1, i))
                    L(tt_(Ss[:, i], Ss[:, i], St[:, i], ALU.add))
                    tt_(St[:, i], Ss[:, i], smp(Rs, i), ALU.mult).then_inc(sst_ready, 1)
                dve.sem_inc(sst_done, 1)

            def state_3():
                for i in range(4):
                    filled(dve, ("sE", 2, i))
                    empties(tt_(St[:, i], bank_s(("sE", 2, i)), dup, ALU.mult), ("sE", 2, i))
                    evacuated(dve, ("sE", 2, i))
                    L(tv.reduce_sum(F_y[:, i, SEQ:T], St[:, i], axis=AX))
                dve.sem_inc(y_done[2], 1)

            def sample_scores():
                dve.wait_ge(cache_used, 64)
                L(tv.tensor_copy(sc_s[0:64, :], pS[0:64, :]))
                sv3 = sc_s[0:64, :].rearrange("p (n k) -> p n k", n=8)
                L(tv.reduce_sum(g64[:, 0:8], sv3, axis=AX))
                cmp = g64b[:, :].rearrange("p (a b) -> p a b", a=8)
                tie = tie64.rearrange("p (a b) -> p a b", a=8)
                gi, gj = bc(g64[:, 0:8].unsqueeze(2), 64, 8, 8), bc(g64[:, 0:8].unsqueeze(1), 64, 8, 8)
                tt_(cmp, gj, gi, ALU.is_gt)
                L(tt_(tie, gj, gi, ALU.is_equal))
                L(tt_(tie, tie, C("lower8", 64, 64).rearrange("p (a b) -> p a b", a=8), ALU.mult))
                L(tt_(cmp, cmp, tie, ALU.add))
                L(tv.reduce_sum(g64[:, 8:16], cmp, axis=AX))
                L(ts_(g64[:, 16:24], g64[:, 8:16], 2.5, -BIG, ALU.is_gt, ALU.mult))
                L(tt_(sv3, sv3, bc(g64[:, 16:24].unsqueeze(2), 64, 8, 256), ALU.add))
                L(tv.reduce_max(g64[:, 36:37], sc_s[0:64, :], axis=AX))
                L(tt_(g64[:, 36:37], g64[:, 36:37], g64[:, 32:33], ALU.max))
                ts_(g64[:, 33:34], g64[:, 36:37], -SCALE, None, ALU.mult).then_inc(s_max, 1)

            def sample_softmax():
                dve.wait_ge(s_exp, 1)
                L(tt_(g64[:, 37:38], g64[:, 34:35], g64[:, 35:36], ALU.add))
                L(tv.reciprocal(g64[:, 37:38], g64[:, 37:38]))
                L(tt_(g64[:, 38:39], g64[:, 35:36], g64[:, 37:38], ALU.mult))
                L(ts_(g64b[:, :], ident[0:64, 0:64], g64[:, 38:39], None, ALU.mult))
                ts_(sc_s[0:64, :], sc_s[0:64, :], g64[:, 37:38], None, ALU.mult).then_inc(s_prob, 1)

            def sample_output():
                filled(dve, ("OT",))
                ov = bank(("OT",))[:, 0:8 * NB].rearrange("p (c b r) -> p c b r", c=4, r=2)
                tv.tensor_copy(cat[0:64, 4:8, SEQ:T], ov[0:64, :, :, 0])
                empties(tv.tensor_copy(cat[64:P, 4:8, SEQ:T], ov[64:P, :, :, 1]), ("OT",))

            def slots(t, kind, rd, r0=None):
                r0 = rd if r0 is None else r0
                first = uses_before(t, kind, r0)
                col = bass.ds(rd * RS, RS)
                shared = kind == 1 and (t == 1 or r0 >= SHARED0)
                mine = [s for s in range(RS) if not (shared and s in SHARE)]
                if kind == 1:
                    if shared and (t, r0) != (0, SHARED0):
                        dve.wait_ge(diag_ready, rd * len(SHARE) + len(SHARE) * shared_round(t, 0))
                    L(tv.tensor_copy(w8[:], wgt[:, col]))
                    if shared:
                        dve.sem_inc(w8_ready, 1)
                for n, s in enumerate(mine):
                    dve.wait_ge(gathered[s], rd * 16 + 16 * (first + 1))
                    if kind == 0:
                        tv.tensor_tensor_reduce(out=ring[:, s, :], in0=ring[:, s, :], in1=xf[:, t, :], scale=1.0,
                                                scalar=0.0, op0=ALU.mult, op1=ALU.add,
                                                accum_out=act8[:, s:s + 1]).then_inc(row_used[s], 1)
                    else:
                        acc = (hb, xf)[n % 2][:, t, :]
                        if n >= 2:
                            dve.wait_ge(row_used[mine[n - 2]], rd + (first + 1))
                        stt(acc, ring[:, s, :], w8[:, s:s + 1], acc, ALU.mult, ALU.add).then_inc(row_used[s], 1)
                if kind == 0:
                    dve.wait_ge(row_used[RS - 1], rd + (first + 1))
                    L(tv.tensor_copy(actv[:, col], act8[:, 0:RS]))
                else:
                    dve.wait_ge(row_used[mine[-2]], rd + (first + 1))
                    dve.wait_ge(row_used[mine[-1]], rd + (first + 1))

            def loop(t, kind, r0, r1):
                n0 = ch.n
                with dve.Fori(r0, r1) as rd:
                    ch.base, ch.n = rd + (n0 - r0), 0
                    slots(t, kind, rd, r0)
                    assert ch.n == 1
                ch.base, ch.n = 0, n0 + (r1 - r0)

            def start_values(t):
                dve.wait_ge(gelu_done, t + 1)
                L(tt_(wgt[:], actv[:], gate[:, t, :], ALU.mult))
                L(tv.memset(xf[:, t, :], 0.0))

            def end_values(t):
                L(tt_(hb[:, t, :], hb[:, t, :], xf[:, t, :], ALU.add))
                dve.wait_ge(row_used[SHARE[-1]], (32, 66)[t])
                L(tt_(hb[:, t, :], hb[:, t, :], pS[:, 0:D_MODEL], ALU.add))
                dve.sem_inc(acc_ready, 1)

            def finish(t):
                n = tok[t][1]
                dve.wait_ge(y_sq, (1, 3, 2)[t])
                dve.wait_ge(gain_in, 32)
                L(tv.reciprocal(st4[0:n, 12:13], st4[0:n, 12:13]))
                stt(xf[0:n, t, :], hb[0:n, t, :], st4[0:n, 12:13], gain[0:n, :], ALU.mult, ALU.mult).then_inc(y_ready, 1)

            def samples_u():
                for b in range(NB):
                    dve.wait_ge(gathered[b], 16 * 57)
                    for hf in range(2):
                        job = ("xb", b, hf)
                        filled(dve, job)
                        part = ring[:, b, hf * 512:(hf + 1) * 512]
                        empties(tv.tensor_tensor_reduce(out=part, in0=part, in1=bank(job)[:, :], scale=1.0, scalar=0.0,
                                                        op0=ALU.mult, op1=ALU.add,
                                                        accum_out=act8[:, hf * NB + b:hf * NB + b + 1]), job)
                        evacuated(dve, job)
                    dve.sem_inc(row_used[b], 1)
                L(tt_(actS[:], act8[:, 0:NB], act8[:, NB:2 * NB], ALU.add))
                dve.sem_inc(u_done, 1)

            def samples_weights():
                dve.wait_ge(gelu_done, 3)
                L(tv.memset(wSz[:], 0.0))
                L(tt_(actS[:], actS[:], gTs[:], ALU.mult))
                tv.tensor_copy(wSz[:].rearrange("p a b -> p (a b)")[:, 0:64:9], actS[:]).then_inc(w_ready, 1)

            def gates_T():
                filled(dve, ("jT",))
                tv.tensor_copy(idxTs[:], bank(("jT",))[:, 0:NB])
                empties(tv.tensor_copy(gTs[:], bank(("jT",))[:, NB:2 * NB]), ("jT",))
                evacuated(dve, ("jT",))
                dve.sem_inc(sT_ready, 1)

            between0 = [
                [(state_0,), (att_a, 2)],
                [(att_b, 2), (state_1,)],
                [(att_c, 2), (att_a, 3), (sample_scores,)],
                [(att_b, 3), (state_2,), (sample_softmax,)],
                [(att_c, 3), (att_a, 4)],
                [(att_b, 4), (state_3,)],
                [(att_c, 4), (att_a, 5)],
                [(att_b, 5)],
                [],
                [(att_c, 5), (a_matrices, 1, (0, 1, 2)), (level_masks, 1)],
                [(level, 1, 1), (level_masks, 2)],
                [(level, 1, 2), (level_masks, 3)],
                [(level, 1, 3), (level_masks, 4)],
                [(level, 1, 4), (level_masks, 5)],
                [(level, 1, 5)],
                [(a_matrices, 1, (3, 4))],
                [(chunk, 2)],
                [(chunk, 3)],
                [(y_inner, 1)],
                [(y_post, 1)],
                [(sample_output,), (y_post, 2)],
                [(residual, 1, 0), (residual, 2, 0)],
                [(residual, 1, 1), (residual, 2, 1)],
                [(norm, 1), (norm, 2)],
                [(xfT_copy, 1), (xfT_copy, 2)],
                [(rank_halves, 1, 0)],
                [(rank_halves, 1, 1)],
                [(rank_halves, 1, 2)],
                [(rank_halves, 1, 3)],
                [(rank_sums, 1)],
                [(route, 1)],
                [],
            ]
            for n, steps in enumerate(between0):
                kind, rd = n // 16, n % 16
                if n == 16:
                    start_values(0)
                slots(0, kind, rd)
                if n == 15:
                    dve.sem_inc(u_done, 1)
                for step, *args in steps:
                    step(*args)
            end_values(0)
            loop(1, 0, 0, 2)
            finish(0)
            loop(1, 0, 2, 16)
            dve.sem_inc(u_done, 1)
            start_values(1)
            for n, steps in enumerate([[(rank_halves, 2, 0)], [(rank_halves, 2, 1)], [(rank_halves, 2, 2)],
                                       [(rank_halves, 2, 3)], [(rank_sums, 2)], [(route, 2)], [(gates_T,)],
                                       [(samples_u,)], [(samples_weights,)], []]):
                slots(1, 1, n)
                for step, *args in steps:
                    step(*args)
            loop(1, 1, 10, 12)
            dve.wait_ge(row_used[NB - 1], 60)
            L(tt_(hb[0:NB, 2, :], hb[0:NB, 2, :], pS[0:NB, 1024:2048], ALU.add))
            dve.sem_inc(acc_ready, 1)
            loop(1, 1, 12, 14)
            finish(2)
            loop(1, 1, 14, 16)
            end_values(1)
            finish(1)


_OUTS = [("y_prompt", (SEQ, D_MODEL)), ("y_sample", (NB, D_MODEL)), ("k_prompt", (SEQ, W)), ("v_prompt", (SEQ, W)),
         ("wkv_prompt", (NH, DH, DH)), ("shiftT", (P, NF * (NB + 1))), ("k_sample", (NB, W)), ("v_sample", (NB, W)),
         ("wkv_sample", (P, NP4 * NB * DH))]


def kernel(**x):
    import concourse.bacc as bacc
    from concourse.bass_utils import run_bass_kernel_spmd

    x = {k: np.asarray(v) for k, v in x.items()}

    def feat(v):
        return v.reshape(-1, P).T

    ins = {
        "x_prompt": x["x_prompt"], "x_sample": x["x_sample"].reshape(NB, D_MODEL),
        "const": constants(), "const8": constants8(),
        "prm": np.concatenate([feat(x[n].reshape(-1)) for n in
                               ("mu_shift", "w0", "a0", "k_k", "k_a", "r_k", "gn_gain", "gn_bias", "norm_mix")], 1),
        "pages": x["page_table"].astype(np.int32).reshape(1, NB * NPAGE),
        "w_in": x["w_in"][0], "w_out": x["w_out"][0], "w_pq": x["w_pq"][0],
        "lora": np.concatenate([np.concatenate([x["w_decay_up"][0], x["w_aaa_up"][0]], 0), x["w_gate_up"][0]], 1),
        "shiftT": x["state_shift"][0].reshape(NB, NF, P).transpose(2, 1, 0).reshape(P, NF * NB),
        "state_wkv": x["state_wkv"][0].reshape(NB, NP4, 2, DH, DH).transpose(2, 4, 1, 0, 3).reshape(P, NP4 * NB * DH),
        "cache_k": x["cache_k"][0].reshape(N_POOL, PAGE, 4, P).transpose(0, 3, 2, 1).reshape(N_POOL, P, 4 * PAGE),
        "cache_v": x["cache_v"][0].reshape(N_POOL, PAGE, W),
        "subkT": x["peer_sub_keys"][0].transpose(2, 0, 1),
        "expert_u": x["expert_u"][0], "expert_v": x["expert_v"][0],
        "norm_ffn": x["norm_ffn"][0], "norm_final": x["norm_final"],
    }
    nc = bacc.Bacc("TRN2", target_bir_lowering=False, num_devices=1)
    arrays = {f"in_{n}": np.ascontiguousarray(a) for n, a in ins.items()}
    A = {n: nc.dram_tensor(f"in_{n}", arrays[f"in_{n}"].shape, mybir.dt.from_np(a.dtype), kind="ExternalInput").ap()
         for n, a in ins.items()}
    O = {n: nc.dram_tensor(f"out_{n}", shape, F32, kind="ExternalOutput").ap() for n, shape in _OUTS}
    step_kernel(nc, A, O)
    r = run_bass_kernel_spmd(nc, [arrays], core_ids=[0]).results[0]
    o = {n: r[f"out_{n}"] for n, _ in _OUTS}
    shift = o["shiftT"].reshape(P, NF, NB + 1).transpose(2, 1, 0).reshape(NB + 1, W_RWKV_IN)
    wkv = o["wkv_sample"].reshape(2, DH, NP4, NB, DH).transpose(3, 2, 0, 4, 1).reshape(1, NB, NH, DH, DH)
    return (o["y_prompt"].reshape(1, SEQ, D_MODEL), o["y_sample"].reshape(NB, 1, D_MODEL),
            o["k_prompt"].reshape(1, 1, SEQ, NH, DH), o["v_prompt"].reshape(1, 1, SEQ, NH, DH),
            o["wkv_prompt"].reshape(1, 1, NH, DH, DH), shift[0:1].reshape(1, 1, W_RWKV_IN),
            o["k_sample"].reshape(1, NB, 1, NH, DH), o["v_sample"].reshape(1, NB, 1, NH, DH),
            wkv, shift[1:].reshape(1, NB, W_RWKV_IN))
```
